# Optimizing a Trainium2 kernel written in Bass

```python
import jax, jax.numpy as jnp
from jax import lax
import numpy as np
import math

D_MODEL = 1024
BATCH = 1
SEQ = 256
DEPTH = 2

D_FF = 2816
N_EVEN = (DEPTH + 1) // 2
N_ODD = DEPTH // 2
N_ADA = 9
EPS = 1e-6
NEG_INF = -1e30
Q_BLOCK = 128

CONV_WIDTH = 512
CONV_GROUPS = 8
CONV_TAPS = 3
MLA_HEADS = 8
MLA_NOPE = 64
MLA_ROPE = 32
MLA_V = 64
Q_LORA = 256
KV_LORA = 128
ROPE_THETA = 10000.0
HY_IN = 3 * CONV_WIDTH + Q_LORA + KV_LORA + MLA_ROPE
HY_MIX = CONV_WIDTH + MLA_HEADS * MLA_V
NSA_HEADS = 16
NSA_KV_HEADS = 2
NSA_GROUP = NSA_HEADS // NSA_KV_HEADS
NSA_DK = 64
CMP_BLOCK = 32
CMP_STRIDE = 16
CMP_HID = 128
SLC_BLOCK = 64
N_SEL = 8
WINDOW = 512
FORCE_SCORE = 1e4
NSA_KV_W = 2 * NSA_KV_HEADS * NSA_DK
NSA_IN = NSA_HEADS * NSA_DK + 3 * NSA_KV_W + 3 * NSA_HEADS


def rms_norm(x, g):
    xf = x.astype(jnp.float32)
    y = xf * lax.rsqrt(jnp.mean(xf * xf, axis=-1, keepdims=True) + EPS)
    return (y * g.astype(jnp.float32)).astype(x.dtype)

def modulate(x, g, shift, scale):
    return rms_norm(x, g) * (1 + scale[:, None]) + shift[:, None]

def swiglu(h, w13, w2):
    a, b = jnp.split(h @ w13, 2, axis=-1)
    return (jax.nn.silu(a) * b) @ w2

def masked_softmax(s, mask):
    s = jnp.where(mask, s.astype(jnp.float32), NEG_INF)
    m = jnp.max(s, axis=-1, keepdims=True)
    p = jnp.exp(s - m) * mask
    return p / jnp.maximum(jnp.sum(p, axis=-1, keepdims=True), 1e-20)

def rope_tables(positions):
    half = MLA_ROPE // 2
    inv = ROPE_THETA ** (-jnp.arange(half, dtype=jnp.float32) / half)
    ang = positions.astype(jnp.float32)[..., None] * inv
    return jnp.cos(ang), jnp.sin(ang)

def apply_rope(t, cos, sin):
    half = t.shape[-1] // 2
    t1 = t[..., :half].astype(jnp.float32)
    t2 = t[..., half:].astype(jnp.float32)
    return jnp.concatenate([t1 * cos - t2 * sin, t1 * sin + t2 * cos], axis=-1).astype(t.dtype)

def to_blocks(t, nqb):
    return jnp.moveaxis(t.reshape(t.shape[0], nqb, Q_BLOCK, *t.shape[2:]), 1, 0)

def from_blocks(o):
    o = jnp.moveaxis(o, 0, 1)
    return o.reshape(o.shape[0], o.shape[1] * o.shape[2], *o.shape[3:])

def short_conv(u, conv_w):
    ch = u.shape[-1]
    return lax.conv_general_dilated(
        u, conv_w[:, None, :], window_strides=(1,), padding=((CONV_TAPS - 1, 0),),
        dimension_numbers=('NWC', 'WIO', 'NWC'), feature_group_count=ch)

def mla_attention(q_nope, q_rope, k_nope, k_rope, v):
    S = q_nope.shape[1]
    nqb = S // Q_BLOCK
    scale = (MLA_NOPE + MLA_ROPE) ** -0.5
    kpos = jnp.arange(S)

    def block(args):
        i, qn, qr = args
        s = (jnp.einsum('bqhd,bkhd->bhqk', qn, k_nope)
             + jnp.einsum('bqhd,bkd->bhqk', qr, k_rope)) * scale
        qpos = i * Q_BLOCK + jnp.arange(Q_BLOCK)
        p = masked_softmax(s, kpos[None, :] <= qpos[:, None])
        return jnp.einsum('bhqk,bkhd->bqhd', p.astype(v.dtype), v)

    o = lax.map(block, (jnp.arange(nqb), to_blocks(q_nope, nqb), to_blocks(q_rope, nqb)))
    return from_blocks(o)

def hybrid_conv_mla(h, cos, sin, w_in, conv_w, q_norm, kv_norm, w_uq, w_ukv, w_out):
    B, S, _ = h.shape
    z = h @ w_in
    cw = CONV_WIDTH
    u, gate_c, gate_b, cq, ckv, kr = jnp.split(
        z, [cw, 2 * cw, 3 * cw, 3 * cw + Q_LORA, 3 * cw + Q_LORA + KV_LORA], axis=-1)
    y_conv = gate_b * short_conv(gate_c * u, conv_w)
    q = (rms_norm(cq, q_norm) @ w_uq).reshape(B, S, MLA_HEADS, MLA_NOPE + MLA_ROPE)
    q_nope, q_rope = q[..., :MLA_NOPE], apply_rope(q[..., MLA_NOPE:], cos[:, :, None], sin[:, :, None])
    kv = (rms_norm(ckv, kv_norm) @ w_ukv).reshape(B, S, MLA_HEADS, MLA_NOPE + MLA_V)
    k_nope, v = kv[..., :MLA_NOPE], kv[..., MLA_NOPE:]
    k_rope = apply_rope(kr, cos, sin)
    y_att = mla_attention(q_nope, q_rope, k_nope, k_rope, v).reshape(B, S, MLA_HEADS * MLA_V)
    return jnp.concatenate([y_conv, y_att], axis=-1) @ w_out

def nsa_attention(h, w_in, cmp_pe, cmp_w1, cmp_w2, gate_b, w_out):
    B, S, _ = h.shape
    G, R, DK = NSA_KV_HEADS, NSA_GROUP, NSA_DK
    dt = h.dtype
    z = h @ w_in
    qd = NSA_HEADS * DK
    q, kv_c, kv_s, kv_w, g = jnp.split(
        z, [qd, qd + NSA_KV_W, qd + 2 * NSA_KV_W, qd + 3 * NSA_KV_W], axis=-1)
    q = q.reshape(B, S, G, R, DK)
    gates = jax.nn.sigmoid(g + gate_b).reshape(B, S, G, R, 3)
    kv_c = kv_c.reshape(B, S, 2, G, DK)
    kv_s = kv_s.reshape(B, S, 2, G, DK)
    kv_w = kv_w.reshape(B, S, 2, G, DK)

    nc = (S - CMP_BLOCK) // CMP_STRIDE + 1
    cidx = jnp.arange(nc)[:, None] * CMP_STRIDE + jnp.arange(CMP_BLOCK)[None, :]

    def compress(t, pe, w1, w2):
        blk = t[:, cidx] + pe[:, None, :]
        blk = jnp.moveaxis(blk, 3, 2).reshape(B, nc, G, CMP_BLOCK * DK)
        return jax.nn.silu(blk @ w1) @ w2

    k_cmp = compress(kv_c[:, :, 0], cmp_pe[0], cmp_w1[0], cmp_w2[0])
    v_cmp = compress(kv_c[:, :, 1], cmp_pe[1], cmp_w1[1], cmp_w2[1])
    cmp_end = jnp.arange(nc) * CMP_STRIDE + CMP_BLOCK - 1

    ns = S // SLC_BLOCK
    n_sel = min(N_SEL, ns)
    cs = jnp.arange(nc)[:, None] * CMP_STRIDE
    ss = jnp.arange(ns)[None, :] * SLC_BLOCK
    overlap = jnp.clip(jnp.minimum(cs + CMP_BLOCK, ss + SLC_BLOCK) - jnp.maximum(cs, ss), 0, None)
    agg = overlap.astype(jnp.float32) / CMP_BLOCK
    blk_idx = jnp.arange(ns)
    k_slc = kv_s[:, :, 0].reshape(B, ns, SLC_BLOCK, G, DK).transpose(0, 3, 1, 2, 4)
    v_slc = kv_s[:, :, 1].reshape(B, ns, SLC_BLOCK, G, DK).transpose(0, 3, 1, 2, 4)
    bi = jnp.arange(B)[:, None, None, None]
    gi = jnp.arange(G)[None, :, None, None]

    pad = ((0, 0), (WINDOW, 0), (0, 0), (0, 0))
    k_win = jnp.pad(kv_w[:, :, 0], pad)
    v_win = jnp.pad(kv_w[:, :, 1], pad)
    scale = DK ** -0.5
    nqb = S // Q_BLOCK

    def block(args):
        i, qb, gb = args
        t = i * Q_BLOCK + jnp.arange(Q_BLOCK)
        s_c = jnp.einsum('bqgrd,bngd->bgrqn', qb, k_cmp) * scale
        p_c = masked_softmax(s_c, cmp_end[None, :] <= t[:, None])
        o_c = jnp.einsum('bgrqn,bngd->bqgrd', p_c.astype(dt), v_cmp)
        imp = jnp.einsum('bgrqn,nj->bgqj', p_c, agg)
        cur = t // SLC_BLOCK
        forced = ((blk_idx[None, :] == 0) | (blk_idx[None, :] == cur[:, None])
                  | (blk_idx[None, :] == cur[:, None] - 1))
        causal_blk = blk_idx[None, :] * SLC_BLOCK <= t[:, None]
        imp = jnp.where(forced, FORCE_SCORE, jnp.where(causal_blk, imp, NEG_INF))
        _, sel = lax.top_k(imp, n_sel)
        ks = k_slc[bi, gi, sel].reshape(B, G, Q_BLOCK, n_sel * SLC_BLOCK, DK)
        vs = v_slc[bi, gi, sel].reshape(B, G, Q_BLOCK, n_sel * SLC_BLOCK, DK)
        kpos_s = (sel[..., None] * SLC_BLOCK + jnp.arange(SLC_BLOCK)).reshape(B, G, Q_BLOCK, -1)
        s_s = jnp.einsum('bqgrd,bgqkd->bgrqk', qb, ks) * scale
        p_s = masked_softmax(s_s, kpos_s[:, :, None] <= t[:, None])
        o_s = jnp.einsum('bgrqk,bgqkd->bqgrd', p_s.astype(dt), vs)
        kw = lax.dynamic_slice_in_dim(k_win, i * Q_BLOCK, WINDOW + Q_BLOCK, axis=1)
        vw = lax.dynamic_slice_in_dim(v_win, i * Q_BLOCK, WINDOW + Q_BLOCK, axis=1)
        kpos_w = i * Q_BLOCK - WINDOW + jnp.arange(WINDOW + Q_BLOCK)
        mask_w = ((kpos_w[None, :] <= t[:, None]) & (kpos_w[None, :] > t[:, None] - WINDOW)
                  & (kpos_w[None, :] >= 0))
        s_w = jnp.einsum('bqgrd,bkgd->bgrqk', qb, kw) * scale
        p_w = masked_softmax(s_w, mask_w)
        o_w = jnp.einsum('bgrqk,bkgd->bqgrd', p_w.astype(dt), vw)
        return gb[..., 0:1] * o_c + gb[..., 1:2] * o_s + gb[..., 2:3] * o_w

    o = lax.map(block, (jnp.arange(nqb), to_blocks(q, nqb), to_blocks(gates, nqb)))
    return from_blocks(o).reshape(B, S, NSA_HEADS * DK) @ w_out

def first_inputs(seed: int = 0) -> dict:
    key = jax.random.key(seed)
    ks = jax.random.split(key, 24)
    nrm = lambda k, shape, s: jax.random.normal(k, shape, jnp.float32) * s
    D = D_MODEL
    return {
        "x": nrm(ks[0], (BATCH, SEQ, D), 1.0),
        "c": nrm(ks[1], (BATCH, D), 1.0),
        "positions": (jnp.arange(SEQ, dtype=jnp.int32)[None, :]
                      + jax.random.randint(ks[2], (BATCH, 1), 0, 1024, dtype=jnp.int32)),
        "ada_w": nrm(ks[3], (DEPTH, D, N_ADA * D), 0.5 * D ** -0.5),
        "ada_b": nrm(ks[4], (DEPTH, N_ADA * D), 0.02),
        "norm_g": 1.0 + nrm(ks[5], (DEPTH, 3, D), 0.02),
        "final_g": 1.0 + nrm(ks[6], (D,), 0.02),
        "ff_w13": nrm(ks[7], (DEPTH, 2, D, 2 * D_FF), D ** -0.5),
        "ff_w2": nrm(ks[8], (DEPTH, 2, D_FF, D), D_FF ** -0.5),
        "hy_w_in": nrm(ks[9], (N_EVEN, D, HY_IN), D ** -0.5),
        "hy_conv_w": nrm(ks[10], (N_EVEN, CONV_TAPS, CONV_WIDTH), CONV_TAPS ** -0.5),
        "hy_q_norm": 1.0 + nrm(ks[11], (N_EVEN, Q_LORA), 0.02),
        "hy_kv_norm": 1.0 + nrm(ks[12], (N_EVEN, KV_LORA), 0.02),
        "hy_w_uq": nrm(ks[13], (N_EVEN, Q_LORA, MLA_HEADS * (MLA_NOPE + MLA_ROPE)), Q_LORA ** -0.5),
        "hy_w_ukv": nrm(ks[14], (N_EVEN, KV_LORA, MLA_HEADS * (MLA_NOPE + MLA_V)), KV_LORA ** -0.5),
        "hy_w_out": nrm(ks[15], (N_EVEN, HY_MIX, D), HY_MIX ** -0.5),
        "nsa_w_in": nrm(ks[16], (N_ODD, D, NSA_IN), D ** -0.5),
        "nsa_cmp_pe": nrm(ks[17], (N_ODD, 2, CMP_BLOCK, NSA_DK), 0.1),
        "nsa_cmp_w1": nrm(ks[18], (N_ODD, 2, CMP_BLOCK * NSA_DK, CMP_HID), (CMP_BLOCK * NSA_DK) ** -0.5),
        "nsa_cmp_w2": nrm(ks[19], (N_ODD, 2, CMP_HID, NSA_DK), CMP_HID ** -0.5),
        "nsa_gate_b": nrm(ks[20], (N_ODD, 3 * NSA_HEADS), 0.1),
        "nsa_w_out": nrm(ks[21], (N_ODD, NSA_HEADS * NSA_DK, D), (NSA_HEADS * NSA_DK) ** -0.5),
    }

def first_block(x, c, positions, ada_w, ada_b, norm_g, final_g, ff_w13, ff_w2,
              hy_w_in, hy_conv_w, hy_q_norm, hy_kv_norm, hy_w_uq, hy_w_ukv, hy_w_out,
              nsa_w_in, nsa_cmp_pe, nsa_cmp_w1, nsa_cmp_w2, nsa_gate_b, nsa_w_out):
    cos, sin = rope_tables(positions)
    c_act = jax.nn.silu(c)
    for l in range(DEPTH):
        mod = c_act @ ada_w[l] + ada_b[l]
        sh1, sc1, g1, sh2, sc2, g2, sh3, sc3, g3 = jnp.split(mod, N_ADA, axis=-1)
        h = modulate(x, norm_g[l, 0], sh1, sc1)
        x = x + 0.5 * g1[:, None] * swiglu(h, ff_w13[l, 0], ff_w2[l, 0])
        h = modulate(x, norm_g[l, 1], sh2, sc2)
        m = l // 2
        if l % 2 == 0:
            y = hybrid_conv_mla(h, cos, sin, hy_w_in[m], hy_conv_w[m], hy_q_norm[m],
                                hy_kv_norm[m], hy_w_uq[m], hy_w_ukv[m], hy_w_out[m])
        else:
            y = nsa_attention(h, nsa_w_in[m], nsa_cmp_pe[m], nsa_cmp_w1[m], nsa_cmp_w2[m],
                              nsa_gate_b[m], nsa_w_out[m])
        x = x + g2[:, None] * y
        h = modulate(x, norm_g[l, 2], sh3, sc3)
        x = x + 0.5 * g3[:, None] * swiglu(h, ff_w13[l, 1], ff_w2[l, 1])
    return rms_norm(x, final_g)


N_MIXERS = 2
CONV_WIDTH_2 = 31
N_HEADS = 8
HEAD_DIM = 64
QK_WIDTH = N_HEADS * 2 * HEAD_DIM
V_WIDTH = N_HEADS * 2 * HEAD_DIM
RMS_EPS = 1e-6
SUBLN_EPS = 1e-5
LN_EPS = 1e-5
N_CONV_LAYERS = (DEPTH + 1) // 2
N_ATTN_LAYERS = DEPTH // 2


def _rmsnorm(x, g, eps=RMS_EPS):
    xf = x.astype(jnp.float32)
    y = xf * lax.rsqrt(jnp.mean(xf * xf, axis=-1, keepdims=True) + eps)
    return (y * g.astype(jnp.float32)).astype(x.dtype)

def _layernorm(x, g, b, eps=LN_EPS):
    xf = x.astype(jnp.float32)
    mu = jnp.mean(xf, axis=-1, keepdims=True)
    var = jnp.mean(jnp.square(xf - mu), axis=-1, keepdims=True)
    y = (xf - mu) * lax.rsqrt(var + eps)
    return (y * g.astype(jnp.float32) + b.astype(jnp.float32)).astype(x.dtype)

def _half_ffn(x, g_pre, g_post, w_gate, w_up, w_down):
    h = _rmsnorm(x, g_pre)
    f = (jax.nn.silu(h @ w_gate) * (h @ w_up)) @ w_down
    return x + 0.5 * _rmsnorm(f, g_post)

def _conformer_conv(h, w_pw1, b_pw1, w_dw, b_dw, ln_g, ln_b, w_pw2, b_pw2):
    u = h @ w_pw1 + b_pw1
    u = u[..., :D_MODEL] * jax.nn.sigmoid(u[..., D_MODEL:])
    pad = (CONV_WIDTH_2 - 1) // 2
    c = lax.conv_general_dilated(
        u, w_dw[:, None, :].astype(u.dtype),
        window_strides=(1,), padding=[(pad, pad)],
        dimension_numbers=("NWC", "WIO", "NWC"),
        feature_group_count=D_MODEL) + b_dw
    c = jax.nn.silu(_layernorm(c, ln_g, ln_b))
    return c @ w_pw2 + b_pw2

def _lambda_init(layer_idx):
    return 0.8 - 0.6 * math.exp(-0.3 * layer_idx)

def _diff_attention(h, w_qkv, w_o, lq1, lk1, lq2, lk2, subln_g, lambda_init):
    B, S, _ = h.shape
    qkv = h @ w_qkv
    q, k, v = jnp.split(qkv, [QK_WIDTH, 2 * QK_WIDTH], axis=-1)
    q = q.reshape(B, S, N_HEADS, 2, HEAD_DIM)
    k = k.reshape(B, S, N_HEADS, 2, HEAD_DIM)
    v = v.reshape(B, S, N_HEADS, 2 * HEAD_DIM)
    f32 = jnp.float32
    lam = (jnp.exp(jnp.sum(lq1.astype(f32) * lk1.astype(f32)))
           - jnp.exp(jnp.sum(lq2.astype(f32) * lk2.astype(f32))) + lambda_init)
    slopes = 2.0 ** (-8.0 * (jnp.arange(N_HEADS, dtype=f32) + 1.0) / N_HEADS)
    scale = HEAD_DIM ** -0.5
    kpos = jnp.arange(S, dtype=f32)
    nblk = S // Q_BLOCK
    q_blocks = q.reshape(B, nblk, Q_BLOCK, N_HEADS, 2, HEAD_DIM).transpose(1, 0, 2, 3, 4, 5)
    starts = jnp.arange(nblk, dtype=jnp.int32) * Q_BLOCK

    def one_block(args):
        qb, start = args
        s = jnp.einsum("bqhmd,bkhmd->bhmqk", qb, k).astype(f32) * scale
        qpos = start.astype(f32) + jnp.arange(Q_BLOCK, dtype=f32)
        dist = jnp.abs(qpos[:, None] - kpos[None, :])
        s = s - slopes[:, None, None, None] * dist
        p = jax.nn.softmax(s, axis=-1)
        a = p[:, :, 0] - lam * p[:, :, 1]
        return jnp.einsum("bhqk,bkhe->bqhe", a.astype(v.dtype), v)

    o = lax.map(one_block, (q_blocks, starts))
    o = o.transpose(1, 0, 2, 3, 4).reshape(B, S, N_HEADS, 2 * HEAD_DIM)
    o = _rmsnorm(o, subln_g, SUBLN_EPS) * (1.0 - lambda_init)
    return o.reshape(B, S, V_WIDTH) @ w_o

def second_inputs(seed: int = 0) -> dict:
    key = jax.random.key(seed)
    ks = jax.random.split(key, 24)
    D, F, K = D_MODEL, D_FF, CONV_WIDTH_2
    NC, NA = N_CONV_LAYERS, N_ATTN_LAYERS
    nrm = jax.random.normal
    f32 = jnp.float32

    def gain(k, shape):
        return 1.0 + 0.05 * nrm(k, shape, f32)

    def small(k, shape):
        return 0.02 * nrm(k, shape, f32)

    return {
        "x": nrm(ks[0], (BATCH, SEQ, D), f32),
        "ffn_norm_pre": gain(ks[1], (DEPTH, 2, D)),
        "ffn_norm_post": gain(ks[2], (DEPTH, 2, D)),
        "ffn_w_gate": nrm(ks[3], (DEPTH, 2, D, F), f32) * D ** -0.5,
        "ffn_w_up": nrm(ks[4], (DEPTH, 2, D, F), f32) * D ** -0.5,
        "ffn_w_down": nrm(ks[5], (DEPTH, 2, F, D), f32) * F ** -0.5,
        "mix_norm_pre": gain(ks[6], (DEPTH, D)),
        "mix_norm_post": gain(ks[7], (DEPTH, D)),
        "conv_w_pw1": nrm(ks[8], (NC, D, 2 * D), f32) * D ** -0.5,
        "conv_b_pw1": small(ks[9], (NC, 2 * D)),
        "conv_w_dw": nrm(ks[10], (NC, K, D), f32) * K ** -0.5,
        "conv_b_dw": small(ks[11], (NC, D)),
        "conv_ln_g": gain(ks[12], (NC, D)),
        "conv_ln_b": small(ks[13], (NC, D)),
        "conv_w_pw2": nrm(ks[14], (NC, D, D), f32) * D ** -0.5,
        "conv_b_pw2": small(ks[15], (NC, D)),
        "attn_w_qkv": nrm(ks[16], (NA, D, 2 * QK_WIDTH + V_WIDTH), f32) * D ** -0.5,
        "attn_w_o": nrm(ks[17], (NA, V_WIDTH, D), f32) * V_WIDTH ** -0.5,
        "attn_lambda_q1": 0.1 * nrm(ks[18], (NA, HEAD_DIM), f32),
        "attn_lambda_k1": 0.1 * nrm(ks[19], (NA, HEAD_DIM), f32),
        "attn_lambda_q2": 0.1 * nrm(ks[20], (NA, HEAD_DIM), f32),
        "attn_lambda_k2": 0.1 * nrm(ks[21], (NA, HEAD_DIM), f32),
        "attn_subln_g": gain(ks[22], (NA, 2 * HEAD_DIM)),
    }

def second_block(x, ffn_norm_pre, ffn_norm_post, ffn_w_gate, ffn_w_up, ffn_w_down,
              mix_norm_pre, mix_norm_post,
              conv_w_pw1, conv_b_pw1, conv_w_dw, conv_b_dw, conv_ln_g, conv_ln_b,
              conv_w_pw2, conv_b_pw2,
              attn_w_qkv, attn_w_o, attn_lambda_q1, attn_lambda_k1,
              attn_lambda_q2, attn_lambda_k2, attn_subln_g):
    ic = 0
    ia = 0
    for i in range(DEPTH):
        x = _half_ffn(x, ffn_norm_pre[i, 0], ffn_norm_post[i, 0],
                      ffn_w_gate[i, 0], ffn_w_up[i, 0], ffn_w_down[i, 0])
        h = _rmsnorm(x, mix_norm_pre[i])
        if i % N_MIXERS == 0:
            m = _conformer_conv(h, conv_w_pw1[ic], conv_b_pw1[ic], conv_w_dw[ic],
                                conv_b_dw[ic], conv_ln_g[ic], conv_ln_b[ic],
                                conv_w_pw2[ic], conv_b_pw2[ic])
            ic += 1
        else:
            m = _diff_attention(h, attn_w_qkv[ia], attn_w_o[ia],
                                attn_lambda_q1[ia], attn_lambda_k1[ia],
                                attn_lambda_q2[ia], attn_lambda_k2[ia],
                                attn_subln_g[ia], _lambda_init(i))
            ia += 1
        x = x + _rmsnorm(m, mix_norm_post[i])
        x = _half_ffn(x, ffn_norm_pre[i, 1], ffn_norm_post[i, 1],
                      ffn_w_gate[i, 1], ffn_w_up[i, 1], ffn_w_down[i, 1])
    return x


def setup_inputs(seed=0):
    out = dict(first_inputs(seed))
    for name, value in second_inputs(seed + 1).items():
        if name != "x":
            out[name + "_2"] = value
    return out


def reference(
    x, c, positions, ada_w, ada_b, norm_g, final_g, ff_w13, ff_w2, hy_w_in, hy_conv_w,
    hy_q_norm, hy_kv_norm, hy_w_uq, hy_w_ukv, hy_w_out, nsa_w_in, nsa_cmp_pe, nsa_cmp_w1,
    nsa_cmp_w2, nsa_gate_b, nsa_w_out, ffn_norm_pre_2, ffn_norm_post_2, ffn_w_gate_2,
    ffn_w_up_2, ffn_w_down_2, mix_norm_pre_2, mix_norm_post_2, conv_w_pw1_2, conv_b_pw1_2,
    conv_w_dw_2, conv_b_dw_2, conv_ln_g_2, conv_ln_b_2, conv_w_pw2_2, conv_b_pw2_2,
    attn_w_qkv_2, attn_w_o_2, attn_lambda_q1_2, attn_lambda_k1_2, attn_lambda_q2_2,
    attn_lambda_k2_2, attn_subln_g_2,
):
    x = first_block(
        x, c, positions, ada_w, ada_b, norm_g, final_g, ff_w13, ff_w2, hy_w_in, hy_conv_w,
        hy_q_norm, hy_kv_norm, hy_w_uq, hy_w_ukv, hy_w_out, nsa_w_in, nsa_cmp_pe, nsa_cmp_w1,
        nsa_cmp_w2, nsa_gate_b, nsa_w_out,
    )
    return second_block(
        x, ffn_norm_pre_2, ffn_norm_post_2, ffn_w_gate_2, ffn_w_up_2, ffn_w_down_2,
        mix_norm_pre_2, mix_norm_post_2, conv_w_pw1_2, conv_b_pw1_2, conv_w_dw_2, conv_b_dw_2,
        conv_ln_g_2, conv_ln_b_2, conv_w_pw2_2, conv_b_pw2_2, attn_w_qkv_2, attn_w_o_2,
        attn_lambda_q1_2, attn_lambda_k1_2, attn_lambda_q2_2, attn_lambda_k2_2, attn_subln_g_2,
    )


_drawn_inputs = setup_inputs


def setup_inputs(seed=0):
    import zlib

    import numpy as np

    out = dict(_drawn_inputs(seed))
    spreads = {}
    factors = {'norm_g': 3.615,
     'hy_q_norm': 8.0,
     'hy_kv_norm': 8.0,
     'nsa_cmp_pe': 21.264,
     'nsa_gate_b': 23.262,
     'attn_lambda_q1_2': 6.694,
     'attn_lambda_q2_2': 3.944,
     'conv_b_pw1_2': 2.667,
     'conv_ln_b_2': 2.809}
    for name, (base, spread) in spreads.items():
        noise = np.random.default_rng([zlib.crc32(name.encode()), seed]).standard_normal(out[name].shape)
        drawn = base * np.exp(spread * noise) if base else spread * noise
        out[name] = __import__('jax').numpy.asarray(drawn.astype(out[name].dtype))
    for name, factor in factors.items():
        out[name] = (out[name] * factor).astype(out[name].dtype)
    return out
```

```python
import math
from contextlib import ExitStack

import numpy as np

import concourse.bass as bass
from concourse import mybir

F32 = mybir.dt.float32
F32R = mybir.dt.float32r
BF16 = mybir.dt.bfloat16
I32 = mybir.dt.int32
ALU = mybir.AluOpType
ACT = mybir.ActivationFunctionType
AXX = mybir.AxisListType.X

P = 128
T = 256
TT = T // P
D = 1024
KD = D // P
FF = 2816
STEP = 2 * P
NSTEP = FF // STEP
SLAB = 2048
EPS = 1e-6
NADA = 9
PAIR = 4
NPAIR = 2 * NADA * KD // PAIR
NEG = -1e30

LAMBDA_INIT = 0.8 - 0.6 * math.exp(-0.3)

A, B, W = 0, 1, 2


def inv_freq():
    half = 16
    return (np.float32(10000.0) ** (-np.arange(half, dtype=np.float32) / np.float32(half))).astype(np.float32)


VEC = {}


def _columns():
    at = 0
    for name, n in (
        ("c", 8), ("ada_b", 144), ("norm_g", 48), ("final_g", 8), ("hy_conv", 12), ("q_norm", 2), ("kv_norm", 1),
        ("pe", 64), ("ffn_pre", 32), ("ffn_post", 32), ("mix_pre", 16), ("mix_post", 16), ("b_pw1", 16),
        ("w_dw", 248), ("b_dw", 8), ("ln_g", 8), ("ln_b", 8), ("b_pw2", 8), ("subln", 1), ("lam", 4),
        ("gate_b", 48), ("cmp_w2k", 128), ("cmp_w2v", 64),
    ):
        VEC[name] = (at, n)
        at += n
    return at


NVEC = _columns()

CON = {"ident": 0, "causal": 128, "dist": 256, "cmp": 768, "row_ok": 798, "inv": 800, "sign": 801}
NCON = 802
NCMP = (T - 32) // 16 + 1
SLOPES = [2.0 ** (-8.0 * (h + 1.0) / 8) for h in range(8)]


def constants():
    c = np.zeros((P, NCON), np.float32)
    r = np.arange(P)
    c[:, 0:128] = np.eye(P)
    c[:, 128:256] = np.where(r[None, :] <= r[:, None], 0.0, NEG)
    for t in range(TT):
        q = t * P + r
        c[:, 256 + t * T:256 + (t + 1) * T] = np.abs(q[:, None] - np.arange(T)[None, :])
        end = np.arange(NCMP) * 16 + 31
        c[:, 768 + t * NCMP:768 + (t + 1) * NCMP] = np.where(end[None, :] <= q[:, None], 0.0, NEG)
        c[:, 798 + t] = q >= 31
    c[:, 800] = inv_freq()[r % 16]
    c[:, 801] = np.where(r % 32 < 16, -1.0, 1.0)
    return c


class Count(dict):

    def take(self, name, n=1):
        v = self.get(name, 0)
        self[name] = v + n
        return v


def program(nc, x_in, pos_in, vec_in, con_in, ada_in, stream_in, out):
    ctx = ExitStack()
    with ctx:
        def sb(name, shape, dt=F32):
            return ctx.enter_context(nc.sbuf_tensor(name, shape, dt))

        def ps(name, shape):
            return ctx.enter_context(nc.psum_tensor(name, shape, F32))

        def sem(name):
            return ctx.enter_context(nc.semaphore(name))

        raw = [sb(f"raw{s}", [P, SLAB]) for s in range(3)]
        hi = [sb(f"hi{s}", [P, SLAB], F32R) for s in range(3)]
        lo = [sb(f"lo{s}", [P, SLAB], F32R) for s in range(3)]
        ada_raw = sb("ada_raw", [P, 2, 2 * SLAB])
        ada_acc = sb("ada_acc", [P, PAIR * P])
        x = sb("x", [P, KD, T])
        hf = sb("hf", [P, KD, T])
        h_hi = sb("h_hi", [P, KD, T], F32R)
        h_lo = sb("h_lo", [P, KD, T], F32R)
        silu = sb("silu", [P, 2 * T])
        gf = sb("gf", [P, 2 * T])
        g_hi = sb("g_hi", [P, 2 * T], F32R)
        g_lo = sb("g_lo", [P, 2 * T], F32R)
        z_hi = sb("z_hi", [P, 2 * T], F32R)
        z_lo = sb("z_lo", [P, 2 * T], F32R)
        rstd = sb("rstd", [P, T])
        var = sb("var", [P, T])
        vec = sb("vec", [P, NVEC])
        cact = sb("cact", [P, 8])
        mod = sb("mod", [P, 2 * NADA * KD])
        gain = sb("gain", [P, KD])
        gate = sb("gate", [P, KD])
        ident = sb("ident", [P, P])
        ones = {n: sb(f"ones{n}", [P, P]) for n in (1024, 256, 128)}
        one = sb("one", [P, 2])
        ident_b = sb("ident_b", [P, P], BF16)
        causal_b = sb("causal_b", [P, P], BF16)
        dist_b = sb("dist_b", [P, TT, T], BF16)
        cmp_b = sb("cmp_b", [P, TT, NCMP], BF16)
        slope_b = sb("slope_b", [P, 8, P], BF16)
        zero_b = sb("zero_b", [P, 512], BF16)
        small = sb("small", [P, 208])
        pe_hi = sb("pe_hi", [P, 64], F32R)
        pe_lo = sb("pe_lo", [P, 64], F32R)
        hid = sb("hid", [P, 2, 2 * NCMP])
        hid_b = sb("hid_b", [P, 2])
        qT = sb("qT", [P, KD, T])
        kT = sb("kT", [P, KD, T])
        vt = sb("vt", [P, TT, D])
        ot = sb("ot", [P, TT, D])
        pr = sb("pr", [P, 3, 2 * T])
        pT = sb("pT", [P, 2, 2 * T])
        nmax = sb("nmax", [P, 4, 4])
        sums = sb("sums", [P, 2, 8])
        rec = sb("rec", [P, 8])
        gates = sb("gates", [P, TT, 48])

        Y = ps("Y", [P, KD, T])
        AB = ps("AB", [P, 2, 512])
        M = ps("M", [P, 512])
        N = ps("N", [P, 512])

        x_loaded = sem("x_loaded")
        vec_loaded = sem("vec_loaded")
        con_loaded = sem("con_loaded")
        pos_loaded = sem("pos_loaded")
        raw_in = [sem(f"raw_in{s}") for s in range(3)]
        hi_done = [sem(f"hi_done{s}") for s in range(3)]
        lo_done = [sem(f"lo_done{s}") for s in range(3)]
        used = [sem(f"used{s}") for s in range(3)]
        ada_in_ = [sem(f"ada_in{s}") for s in range(2)]
        ada_mac = sem("ada_mac")
        ada_cols = sem("ada_cols")
        ada_mod = sem("ada_mod")
        act_ready = sem("act_ready")
        const_ready = sem("const_ready")
        x_new = sem("x_new")
        sq_ready = sem("sq_ready")
        stat_ready = sem("stat_ready")
        u_ready = sem("u_ready")
        hh_ready = sem("hh_ready")
        h_ready = sem("h_ready")
        silu_done = sem("silu_done")
        gf_done = sem("gf_done")
        ghi_done = sem("ghi_done")
        glo_done = sem("glo_done")
        dve_link = sem("dve_link")
        act_link = sem("act_link")
        stored = sem("stored")
        rope_in = sem("rope_in")
        rope_ready = sem("rope_ready")
        res_ready = sem("res_ready")
        read_act = sem("read_act")
        read_dve = sem("read_dve")
        u_copied = sem("u_copied")
        cu_done = sem("cu_done")
        yc_done = sem("yc_done")
        lat_u = sem("lat_u")
        lat_hi = sem("lat_hi")
        lat_ready = sem("lat_ready")
        s_ready = sem("s_ready")
        m_ready = sem("m_ready")
        p_ready = sem("p_ready")
        t_ready = sem("t_ready")
        pt_ready = sem("pt_ready")
        pv_done = sem("pv_done")
        o_read = sem("o_read")
        ot_ready = sem("ot_ready")
        turned = sem("turned")
        cmp_hi = sem("cmp_hi")
        cmp_in = sem("cmp_in")
        hid_ready = sem("hid_ready")
        kt_zeroed = sem("kt_zeroed")
        gate_in = sem("gate_in")
        gate_ready = sem("gate_ready")
        dw_done = sem("dw_done")
        mean_ready = sem("mean_ready")
        cen_ready = sem("cen_ready")
        ln_u = sem("ln_u")
        ln_silu = sem("ln_silu")
        lam_in = sem("lam_in")
        lam_exp = sem("lam_exp")

        def v(name, i=0, n=1, rows=slice(None)):
            at = VEC[name][0] + i
            return vec[rows, at:at + n]

        def modv(layer, j, k=0, n=1):
            at = (layer * NADA + j) * KD + k
            return mod[:, at:at + n]

        def mm3(out_, w_hi, w_lo, r_hi, r_lo, start, stop, **kw):
            nc.tensor.matmul(out_, w_hi, r_hi, start=start, stop=False, **kw)
            nc.tensor.matmul(out_, w_hi, r_lo, start=False, stop=False, **kw)
            return nc.tensor.matmul(out_, w_lo, r_hi, start=False, stop=stop, **kw)

        block = ctx.enter_context(nc.Block())

        plan = [("begin",)]
        for n in range(6):
            layer, j = divmod(n, 3)
            plan.append(("norm", n))
            plan.append([("ffn", 2 * layer + j // 2), ("hybrid",) if layer == 0 else ("nsa",)][j == 1])
            plan.append(("add", n))
        plan.append(("final",))
        for n in range(6):
            layer, j = divmod(n, 3)
            plan.append(("norm", 6 + n))
            plan.append([("ffn", 4 + 2 * layer + j // 2), ("conformer",) if layer == 0 else ("diff",)][j == 1])
            plan.append(("add", 6 + n))
        plan.append(("end",))

        ADA_FFN = {0: (4, 11), 1: (16, 11), 2: (27, 9)}
        ADA_MIX = (15, 1)
        def score_bank(G):
            return Y[:, 2 * (G % 2):2 * (G % 2) + 2, :].rearrange("p k t -> p (k t)")

        def turn_bank(G):
            return Y[:, 4 + 2 * (G % 2):6 + 2 * (G % 2), :].rearrange("p k t -> p (k t)")

        def out_bank(bt):
            return M if bt % 2 == 0 else N

        cu = ada_raw[:, 1, 0:4 * (T + 2)].rearrange("p (k t) -> p k t", k=4)
        kz = ada_raw[:, 0, :].rearrange("p (h m t) -> p h m t", h=8, m=2)
        upad = ada_raw[:, 0, 0:KD * (T + 30)].rearrange("p (k t) -> p k t", k=KD)
        cos_, sin_ = ot[:, 1, 512:768], ot[:, 1, 768:1024]
        kcz = small[:, 8:8 + 4 * NCMP].rearrange("p (m n) -> p m n", m=2)
        vcz = small[:, 72:72 + 2 * 64]

        def mla_groups():
            gs = []
            for t in range(TT):
                for h in range(0, 8, 2):
                    nk = (t + 1) * P
                    gs.append(dict(
                        units=[(qT[0:96, h + u, t * P:(t + 1) * P], kT[0:96, h + u, 0:nk],
                                [(t * P, ident_b[:, :], causal_b[:, :])]) for u in range(2)],
                        nk=nk, room=T, tiles=t + 1, batch=t, scale=1.0, sums=h,
                        pv=[((h + u) * 64, [vt[:, j, (h + u) * 64:(h + u + 1) * 64] for j in range(t + 1)])
                            for u in range(2)]))
            return gs

        def nsa_groups():
            gs, bt = [], 0
            for t in range(TT):
                for g in range(2):
                    for branch in range(3):
                        if branch == 0:
                            for h in range(0, 8, 4):
                                us = []
                                for u in range(4):
                                    head = g * 8 + h + u
                                    us.append((qT[:, head // 2, t * P:(t + 1) * P],
                                               kcz[:, head % 2, g:g + 2 * (NCMP - 1) + 1:2],
                                               [(0, ident_b[:, :], cmp_b[:, t, :])]))
                                gs.append(dict(units=us, nk=NCMP, room=P, tiles=1, batch=bt, sums=h,
                                               pv=[((h + u) * 64, [vcz[0:NCMP, g * 64:(g + 1) * 64]])
                                                   for u in range(4)]))
                        else:
                            nk = (t + 1) * P
                            for h in range(0, 8, 2):
                                us = []
                                for u in range(2):
                                    head = g * 8 + h + u
                                    us.append((qT[:, head // 2, t * P:(t + 1) * P],
                                               kT[:, 4 * (branch - 1) + 2 * g + head % 2, 0:nk],
                                               [(t * P, ident_b[:, :], causal_b[:, :])]))
                                at = (branch - 1) * P + g * 64
                                gs.append(dict(units=us, nk=nk, room=T, tiles=t + 1, batch=bt, sums=h,
                                               pv=[((h + u) * 64, [vt[:, j, at:at + 64] for j in range(t + 1)])
                                                   for u in range(2)]))
                        bt += 1
            return gs

        def diff_groups():
            gs = []
            for t in range(TT):
                for h in range(8):
                    gs.append(dict(
                        units=[(qT[:, h, t * P:(t + 1) * P], kz[:, h, m, :],
                                [(0, slope_b[:, h, :], dist_b[:, t, :])]) for m in range(2)],
                        nk=T, room=T, tiles=TT, batch=t * 4 + h // 2, sums=(h % 2) * 2,
                        pv=[(((h % 2) * 2 + m) * P, [vt[:, j, h * P:(h + 1) * P] for j in range(TT)])
                            for m in range(2)]))
            return gs


        @block.sync
        def _(sp):
            c = Count()

            def load(slot, slab, n):
                sp.dma_start(raw[slot][:, :], stream_in[bass.ds(slab, 1), :, :].rearrange("a p n -> (a p) n")
                             ).then_inc(raw_in[slot], 16)

            def free(slot, n):
                sp.wait_ge(lo_done[slot], n)

            def next_slab(slot):
                n = c.take(f"slot{slot}")
                if n:
                    free(slot, n)
                load(slot, c.take("slab"), n)

            def load_ada(buf, q, done):
                if done is not None:
                    sp.wait_ge(ada_mac, done)
                sp.dma_start(ada_raw[:, buf, :], ada_in[bass.ds(q, 1), :, :].rearrange("a p n -> (a p) n")
                             ).then_inc(ada_in_[buf], 16)

            def begin():
                sp.dma_start(vec[:, :], vec_in).then_inc(vec_loaded, 16)
                load_ada(0, 0, None)
                sp.dma_start(x[:, :, :], x_in).then_inc(x_loaded, 16)
                load_ada(1, 1, None)
                sp.dma_start(hf[:, :, :].rearrange("p k t -> p (k t)")[:, 0:NCON], con_in).then_inc(con_loaded, 16)
                sp.dma_start(qT[:, 0, :].bitcast(I32), pos_in.partition_broadcast(P)).then_inc(pos_loaded, 16)
                load_ada(0, 2, KD)
                load_ada(1, 3, 2 * KD)

            def ffn(f):
                q0, n_ada = ADA_FFN.get(f, (0, 0))
                s0 = c.take("slab", 3 * NSTEP)
                u = [c.take(f"slot{s}", NSTEP) for s in range(3)]
                for s in (A, B):
                    if u[s]:
                        free(s, u[s])
                    load(s, s0 + s, u[s])
                if n_ada:
                    load_ada(0, q0, KD * q0)

                def steps(lo_i, hi_i, ada):
                    with sp.Fori(lo_i, hi_i) as i:
                        for s in (A, B):
                            free(s, i + u[s])
                            load(s, i * 3 + (s0 - 1 + s), None)
                        free(W, i + (u[W] - 1))
                        load(W, i * 3 + (s0 + 1), None)
                        if ada:
                            load_ada(0, i + q0, i * KD + KD * q0)

                if u[W] == 0:
                    for s in (A, B):
                        free(s, 1)
                        load(s, s0 + 2 + s, None)
                    load(W, s0 + 4, None)
                    if n_ada:
                        load_ada(0, q0 + 1, KD * (q0 + 1))
                    steps(2, NSTEP, True)
                elif n_ada in (0, NSTEP):
                    steps(1, NSTEP, n_ada > 0)
                else:
                    steps(1, n_ada, True)
                    steps(n_ada, NSTEP, False)
                free(W, u[W] + NSTEP - 1)
                load(W, s0 + 3 * NSTEP - 1, None)

            def mixer(n):
                for j in range(n):
                    next_slab(j % 3)

            def hybrid():
                q0, n = ADA_MIX
                load_ada(0, q0, KD * q0)
                mixer(10)
                for q in range(q0 + 1, q0 + n):
                    load_ada(0, q, KD * q)
                for j in range(10, 14):
                    next_slab(j % 3)

            def end():
                sp.wait_ge(x_new, c["x_new"])
                sp.dma_start(out, x[:, :, :]).then_inc(stored, 16)
                sp.wait_ge(stored, 16)

            steps = {"begin": begin, "ffn": ffn, "hybrid": hybrid, "nsa": lambda: mixer(16),
                     "conformer": lambda: mixer(12), "diff": lambda: mixer(16), "end": end,
                     "add": lambda n: c.take("x_new", KD), "final": lambda: c.take("x_new", KD)}
            for kind, *a in plan:
                if kind in steps:
                    steps[kind](*a)

        @block.tensor
        def _(pe):
            c = Count()

            def slab(slot):
                pe.wait_ge(lo_done[slot], c.take(f"slot{slot}") + 1)
                return hi[slot], lo[slot]

            def cols(q):
                pe.wait_ge(ada_mac, q * KD + KD)
                for j in range(PAIR):
                    mm = nc.tensor.matmul(M[:, j:j + 1], ada_acc[:, j * P:(j + 1) * P], one[:, 0:1],
                                          start=True, stop=True)
                mm.then_inc(ada_cols, 1)

            def begin():
                pe.wait_ge(const_ready, 1)
                for q in range(4):
                    cols(q)

            def stat(n_chunks, ones_, base=0):
                s0 = c.take("sq", n_chunks)
                for k in range(n_chunks):
                    pe.wait_ge(sq_ready, s0 + k + 1)
                    mm = nc.tensor.matmul(N[:, 0:T], ones_[:, :], hf[:, base + k, :], start=(k == 0),
                                          stop=(k == n_chunks - 1))
                mm.then_inc(stat_ready, 1)
                c.take("stat")

            def norm(n):
                stat(KD, ones[1024])
                c.take("h", KD)

            def wait_h(k):
                pe.wait_ge(h_ready, c["h"] - KD + k + 1)

            def up(first, slot):
                for cc in range(2):
                    for k in range(KD):
                        if first and cc == 0:
                            wait_h(k)
                        at = k * 2 * P + cc * P
                        mm = mm3(AB[:, slot, cc * T:(cc + 1) * T], hi[slot][:, at:at + P], lo[slot][:, at:at + P],
                                 h_hi[:, k, :], h_lo[:, k, :], k == 0, k == KD - 1)
                mm.then_inc(used[slot], 1)

            def down():
                for n in range(KD):
                    for cc in range(2):
                        at = cc * D + n * P
                        mm = mm3(Y[:, n, :], hi[W][:, at:at + P], lo[W][:, at:at + P],
                                 g_hi[:, cc * T:(cc + 1) * T], g_lo[:, cc * T:(cc + 1) * T], False, False,
                                 skip_group_check=True)
                mm.then_inc(used[W], 1)

            def ffn(f):
                q0, n_ada = ADA_FFN.get(f, (0, 0))
                u = [c.take(f"slot{s}", NSTEP) for s in range(3)]
                g0 = c.take("g", NSTEP)
                pe.wait_ge(lo_done[A], u[A] + 1)
                up(True, A)
                pe.wait_ge(lo_done[B], u[B] + 1)
                up(False, B)
                for b in range(4):
                    nc.tensor.matmul(Y[:, 2 * b:2 * b + 2, :].rearrange("p k t -> p (k t)"), zero_b[:, 0:P],
                                     zero_b[:, :], start=True, stop=False, skip_group_check=True)

                def steps(lo_i, hi_i, ada):
                    with pe.Fori(lo_i, hi_i) as i:
                        if ada:
                            cols(i + (q0 - 1))
                        pe.wait_ge(lo_done[A], i + (u[A] + 1))
                        pe.wait_ge(gf_done, i + g0)
                        up(False, A)
                        pe.wait_ge(lo_done[B], i + (u[B] + 1))
                        up(False, B)
                        pe.wait_ge(lo_done[W], i + u[W])
                        pe.wait_ge(glo_done, i + g0)
                        down()

                if n_ada in (0, NSTEP):
                    steps(1, NSTEP, n_ada > 0)
                else:
                    steps(1, n_ada + 1, True)
                    steps(n_ada + 1, NSTEP, False)
                if n_ada == NSTEP:
                    cols(q0 + NSTEP - 1)
                pe.wait_ge(lo_done[W], u[W] + NSTEP)
                pe.wait_ge(glo_done, g0 + NSTEP)
                down()
                c.take("y")
                c[f"y_slot"] = (W, u[W] + NSTEP)

            def add(n):
                if n >= 6:
                    stat(KD, ones[1024])

            def final():
                stat(KD, ones[1024])

            READERS = {"a": read_act, "d": read_dve, "c": cu_done, "y": yc_done, "h": hid_ready, "m": cmp_in,
                       "g": gate_in, "e": lam_exp}

            def result(*readers):
                o = c.take("res")
                old = c.setdefault("hist", [])
                if o >= 2:
                    for s_, n_ in old[o - 2]:
                        pe.wait_ge(s_, n_)
                old.append([r if isinstance(r, tuple) else (READERS[r], c.take("read_" + r) + 1) for r in readers])
                return AB[:, o % 2, :]

            def halves(bank):
                return [bank[:, 0:T], bank[:, T:2 * T]]

            def all_read():
                pe.wait_ge(read_act, c["read_a"])
                pe.wait_ge(read_dve, c["read_d"])

            def features(slot, outs, first=False):
                w_hi, w_lo = slab(slot)
                for cc in range(2):
                    for k in range(KD):
                        if first and cc == 0:
                            wait_h(k)
                        at = k * 2 * P + cc * P
                        mm = mm3(outs[cc], w_hi[:, at:at + P], w_lo[:, at:at + P], h_hi[:, k, :], h_lo[:, k, :],
                                 k == 0, k == KD - 1)
                return mm.then_inc(used[slot], 1)

            def tokens(slot, outs, n):
                w_hi, w_lo = slab(slot)
                for t in range(TT):
                    for k in range(KD):
                        mm = mm3(outs[t], h_hi[:, k, t * P:(t + 1) * P], h_lo[:, k, t * P:(t + 1) * P],
                                 w_hi[:, k * 2 * P:k * 2 * P + n], w_lo[:, k * 2 * P:k * 2 * P + n],
                                 k == 0, k == KD - 1)
                return mm.then_inc(used[slot], 1)

            def out_product(j0):
                c.take("h", KD)
                for j in range(4):
                    slot = (j0 + j) % 3
                    features(slot, [Y[:, 2 * j, :], Y[:, 2 * j + 1, :]], first=(j == 0))
                c["y_slot"] = (slot, c[f"slot{slot}"])

            def turn(n_chunks):
                for m in range(n_chunks // 2):
                    bank = result((h_ready, c["h"] + KD - n_chunks + 2 * m + 2))
                    for cc in range(2):
                        for t in range(TT):
                            at = (2 * m + cc) * P
                            mm = nc.tensor.transpose(bank[:, cc * T + t * P:cc * T + (t + 1) * P],
                                                     ot[:, t, at:at + P], ident[:, :])
                    mm.then_inc(turned, 1)

            def attention(groups, beside=None):
                g0 = c.take("grp", len(groups))
                b0 = c.take("batch", groups[-1]["batch"] + 1)

                def scores(g):
                    G, gr = g0 + g, groups[g]
                    if G >= 2:
                        pe.wait_ge(p_ready, G - 1)
                    for u, (q_ap, k_ap, bias) in enumerate(gr["units"]):
                        out_ = score_bank(G)[:, u * gr["room"]:u * gr["room"] + gr["nk"]]
                        nc.tensor.matmul(out_, q_ap, k_ap, start=True, stop=not bias)
                        for i, (b_at, l_ap, r_ap) in enumerate(bias):
                            mm = nc.tensor.matmul(out_[:, b_at:b_at + r_ap.shape[-1]], l_ap, r_ap, start=False,
                                                  stop=(i == len(bias) - 1))
                    mm.then_inc(s_ready, 1)

                def transposes(g):
                    G, gr = g0 + g, groups[g]
                    pe.wait_ge(p_ready, G + 1)
                    if G >= 2:
                        pe.wait_ge(pt_ready, G - 1)
                    n = 0
                    for u in range(len(gr["units"])):
                        for t in range(gr["tiles"]):
                            at = u * gr["room"] + t * P
                            mm = nc.tensor.transpose(turn_bank(G)[:, n * P:(n + 1) * P], pr[:, G % 3, at:at + P],
                                                     ident[:, :])
                            n += 1
                    mm.then_inc(t_ready, 1)

                def values(g):
                    G, gr = g0 + g, groups[g]
                    pe.wait_ge(pt_ready, G + 1)
                    bt = b0 + gr["batch"]
                    if bt >= 2:
                        pe.wait_ge(o_read, bt - 1)
                    n = 0
                    for out_at, vs in gr["pv"]:
                        out_ = out_bank(bt)[:, out_at:out_at + vs[0].shape[-1]]
                        for t, v_ap in enumerate(vs):
                            rows_ = v_ap.shape[0]
                            mm = nc.tensor.matmul(out_, pT[0:rows_, G % 2, n * P:(n + 1) * P], v_ap, start=(t == 0),
                                                  stop=(t == len(vs) - 1))
                            n += 1
                    mm.then_inc(pv_done, 1)

                for s_ in range(len(groups) + 2):
                    if s_ < len(groups):
                        scores(s_)
                    if beside and s_ in beside:
                        beside[s_]()
                    if 1 <= s_ <= len(groups):
                        transposes(s_ - 1)
                    if s_ >= 2:
                        values(s_ - 2)

            def hybrid():
                q0, n_ada = ADA_MIX
                features(0, halves(result("a")), first=True)
                features(1, halves(result("a")))
                features(2, halves(result("c")))
                stat(2, ones[256])
                pe.wait_ge(lat_u, 1)
                stat(1, ones[128], 2)
                features(0, halves(result("c")))
                features(1, halves(result("c")))
                for q in range(q0, q0 + n_ada):
                    cols(q)
                w_hi, w_lo = slab(2)
                pe.wait_ge(lat_ready, 2)
                for h in range(0, 8, 2):
                    outs = halves(result("a", "d"))
                    for cc in range(2):
                        for r in range(2):
                            at = r * D + (h + cc) * P
                            mm = mm3(outs[cc], w_hi[:, at:at + P], w_lo[:, at:at + P], g_hi[:, r * T:(r + 1) * T],
                                     g_lo[:, r * T:(r + 1) * T], r == 0, r == 1)
                    mm.then_inc(res_ready if h < 6 else used[2], 1)
                w_hi, w_lo = slab(0)
                for h in range(0, 8, 2):
                    outs = halves(result("a"))
                    for cc in range(2):
                        at = (h + cc) * P
                        mm = mm3(outs[cc], w_hi[:, at:at + P], w_lo[:, at:at + P], z_hi[:, 0:T], z_lo[:, 0:T],
                                 True, True)
                    mm.then_inc(res_ready, 1)
                for t in range(TT):
                    bank = result("d")
                    vh, vl = (s_[:, 0:8 * P].rearrange("p (h n) -> p h n", h=8)[:, :, 64:128] for s_ in (w_hi, w_lo))
                    mm = mm3(bank, z_hi[:, t * P:(t + 1) * P], z_lo[:, t * P:(t + 1) * P], vh, vl, True, True)
                    mm.then_inc(res_ready if t == 0 else used[0], 1)
                all_read()

                def conv_slab(slot, reader):
                    return lambda: features(slot, halves(result(reader)))

                attention(mla_groups(), {0: conv_slab(1, "c"), 1: conv_slab(2, "y"), 2: conv_slab(0, "y")})
                pe.wait_ge(o_read, c["batch"])
                turn(4)
                out_product(10)

            def nsa():
                for j in range(4):
                    features(j % 3, halves(result("a")), first=(j == 0))
                for j in (4, 5):
                    features(j % 3, halves(result("m")))
                for j in (6, 7):
                    features(j % 3, halves(result("a")))
                tokens(8 % 3, halves(result("d")), 2 * P)
                bank = result("g")
                tokens(9 % 3, [bank[:, 0:48], bank[:, 48:96]], 48)
                for kv, slot in ((0, 10 % 3), (1, 11 % 3)):
                    w_hi, w_lo = slab(slot)
                    pe.wait_ge(cmp_in, 3)
                    bank = result("h")
                    th, tl = ((g_hi, g_lo), (z_hi, z_lo))[kv]
                    for n, (r_hi, r_lo) in enumerate((
                            (th[:, :].rearrange("p (g t) -> p t g", g=2), tl[:, :].rearrange("p (g t) -> p t g", g=2)),
                            (pe_hi[:, kv * 32:kv * 32 + 32].rearrange("p (j d) -> p j d", d=2),
                             pe_lo[:, kv * 32:kv * 32 + 32].rearrange("p (j d) -> p j d", d=2)))):
                        for j in range(16):
                            if n == 0:
                                a, b_ = (r[:, 2 * j:2 * j + 16 * (NCMP - 1) + 1:16, :] for r in (r_hi, r_lo))
                                out_ = bank[:, 0:2 * NCMP]
                            else:
                                a, b_ = r_hi[:, j, :], r_lo[:, j, :]
                                out_ = bank[:, 2 * NCMP:2 * NCMP + 2]
                            mm = mm3(out_, w_hi[:, j * P:(j + 1) * P], w_lo[:, j * P:(j + 1) * P], a, b_,
                                     j == 0, j == 15)
                    mm.then_inc(used[slot], 1)
                pe.wait_ge(hid_ready, 2)
                bank = result("a")
                nc.tensor.matmul(bank[:, 0:2 * NCMP], v("cmp_w2k", 0, 128), hid[:, 0, :], start=True, stop=True
                                 ).then_inc(res_ready, 1)
                bank = result("a")
                for g in range(2):
                    mm = nc.tensor.matmul(bank[0:NCMP, g * 64:(g + 1) * 64],
                                          hid[:, 1, :].rearrange("p (n g) -> p g n", g=2)[:, g, :],
                                          v("cmp_w2v", 0, 64), start=True, stop=True)
                mm.then_inc(res_ready, 1)
                all_read()
                attention(nsa_groups())
                pe.wait_ge(o_read, c["batch"])
                turn(8)
                out_product(12)

            def conformer():
                for j in range(8):
                    features(j % 3, halves(result("c")), first=(j == 0))
                for k in range(KD):
                    pe.wait_ge(dw_done, k + 1)
                    mm = nc.tensor.matmul(N[:, 0:T], ones[1024][:, :], qT[:, k, :], start=(k == 0), stop=(k == KD - 1))
                mm.then_inc(mean_ready, 1)
                stat(KD, ones[1024])
                out_product(8)

            def diff():
                for j in range(8):
                    features(j % 3, halves(result("a")), first=(j == 0))
                for j in range(8, 12):
                    tokens(j % 3, halves(result("a")), 2 * P)
                pe.wait_ge(lam_in, 1)
                bank = result("e")
                nc.tensor.matmul(bank[:, 0:2], ones[128][:, :], small[:, 4:6], start=True, stop=True
                                 ).then_inc(res_ready, 1)
                all_read()
                attention(diff_groups())
                pe.wait_ge(ot_ready, TT)
                turn(8)
                out_product(12)

            steps = {"begin": begin, "norm": norm, "ffn": ffn, "add": add, "final": final, "hybrid": hybrid, "nsa": nsa,
                     "conformer": conformer, "diff": diff}
            for kind, *a in plan:
                if kind in steps:
                    steps[kind](*a)

        @block.scalar
        def _(act):
            c = Count()

            def link(ins):
                act_n = c.take("link") + 1
                ins.then_inc(act_link, 1)
                act.wait_ge(act_link, act_n)

            def split(slot, n):
                act.wait_ge(raw_in[slot], n * 16 + 16)
                nc.scalar.activation(hi[slot][:, :], raw[slot][:, :], ACT.Copy).then_inc(hi_done[slot], 1)

            def next_slab(slot):
                n = c.take(f"slot{slot}")
                if n:
                    act.wait_ge(used[slot], n)
                split(slot, n)

            def begin():
                act.wait_ge(vec_loaded, 16)
                nc.scalar.activation(cact[:, :], v("c", 0, 8), ACT.Silu).then_inc(act_ready, 1)
                act.wait_ge(rope_in, 1)
                nc.scalar.activation(sin_, qT[:, 1, :], ACT.Sin, scale=small[:, 3:4])
                nc.scalar.activation(cos_, qT[:, 3, :], ACT.Sin).then_inc(rope_ready, 1)

            def norm(n):
                s0 = c.take("sq", KD)
                u0 = c.take("u", KD)
                c.take("hh", KD)
                for k in range(KD):
                    if n == 0:
                        if k == 0:
                            act.wait_ge(x_loaded, 16)
                            act.wait_ge(const_ready, 2)
                    else:
                        act.wait_ge(x_new, c["x_new"] - KD + k + 1)
                    nc.scalar.activation(hf[:, k, :], x[:, k, :], ACT.Square).then_inc(sq_ready, 1)
                for k in range(KD):
                    act.wait_ge(u_ready, u0 + k + 1)
                    if n < 6:
                        nc.scalar.activation(h_hi[:, k, :], hf[:, k, :], ACT.Identity,
                                             bias=modv(n // 3, 3 * (n % 3), k)).then_inc(hh_ready, 1)
                    else:
                        nc.scalar.activation(h_hi[:, k, :], hf[:, k, :], ACT.Copy).then_inc(hh_ready, 1)

            def g_split(g):
                act.wait_ge(gf_done, g + 1)
                nc.scalar.activation(g_hi[:, :], gf[:, :], ACT.Copy).then_inc(ghi_done, 1)

            def ffn(f):
                u = [c.take(f"slot{s}", NSTEP) for s in range(3)]
                g0 = c.take("g", NSTEP)
                for s in (A, B):
                    if u[s]:
                        act.wait_ge(used[s], u[s])
                    split(s, u[s])

                def step(i, first):
                    for s in (A, B):
                        act.wait_ge(used[s], i + u[s])
                        split(s, i + u[s])
                    nc.scalar.activation(silu[:, :], AB[:, A, :], ACT.Silu).then_inc(silu_done, 1)
                    if not first:
                        act.wait_ge(used[W], i + (u[W] - 1))
                    split(W, i + (u[W] - 1))
                    g_split(i + (g0 - 1))

                first = u[W] == 0
                if first:
                    step(1, True)
                with act.Fori(2 if first else 1, NSTEP) as i:
                    step(i, False)
                act.wait_ge(used[B], u[B] + NSTEP)
                nc.scalar.activation(silu[:, :], AB[:, A, :], ACT.Silu).then_inc(silu_done, 1)
                act.wait_ge(used[W], u[W] + NSTEP - 1)
                split(W, u[W] + NSTEP - 1)
                g_split(g0 + NSTEP - 1)
                c["y_slot"] = (W, u[W] + NSTEP)

            def add(n):
                c.take("x_new", KD)
                if n >= 6:
                    s0 = c.take("sq", KD)
                    slot, value = c["y_slot"]
                    act.wait_ge(used[slot], value)
                    for k in range(KD):
                        bias = v("b_pw2", k) if n == 7 else 0.0
                        nc.scalar.activation(hf[:, k, :], Y[:, k, :], ACT.Square, bias=bias).then_inc(sq_ready, 1)

            def final():
                s0 = c.take("sq", KD)
                for k in range(KD):
                    act.wait_ge(x_new, c["x_new"] - KD + k + 1)
                    nc.scalar.activation(hf[:, k, :], x[:, k, :], ACT.Square).then_inc(sq_ready, 1)
                c.take("x_new", KD)

            def start_mixer():
                c["base"] = [c.get(f"slot{s}", 0) for s in range(3)]

            def ready(j):
                act.wait_ge(used[j % 3], c["base"][j % 3] + j // 3 + 1)

            def passing(n=1):
                act.wait_ge(res_ready, c.take("passing", n) + n)

            def halves(bank):
                return [bank[:, 0:T], bank[:, T:2 * T]]

            def bank():
                return AB[:, c.take("res") % 2, :]

            def read(ins):
                c.take("read_a")
                ins.then_inc(read_act, 1)

            def operand():
                return c.take("hh", KD)

            def attention(groups, beside=None):
                g0 = c.take("grp", len(groups))
                b0 = c.take("batch", groups[-1]["batch"] + 1)
                for s_, gr in enumerate(groups):
                    G, bt = g0 + s_, b0 + gr["batch"]
                    act.wait_ge(m_ready, G + 1)
                    if G >= 3:
                        act.wait_ge(t_ready, G - 2)
                    if gr["sums"] == 0 and bt >= 2:
                        act.wait_ge(o_read, bt - 1)
                    for u in range(len(gr["units"])):
                        at = u * gr["room"]
                        ins = nc.scalar.activation(
                            pr[:, G % 3, at:at + gr["nk"]], score_bank(G)[:, at:at + gr["nk"]], ACT.Exp,
                            bias=nmax[:, G % 4, u:u + 1], accum_out=sums[:, bt % 2, gr["sums"] + u:gr["sums"] + u + 1])
                    ins.then_inc(p_ready, 1)
                    if beside and s_ in beside:
                        beside[s_]()

            def turn(n_chunks, gain_=None, first=0):
                for m in range(n_chunks // 2):
                    bk = bank()
                    act.wait_ge(turned, c.take("turned") + 1)
                    for cc in range(2):
                        k = first + 2 * m + cc
                        scale = 1.0 if gain_ is None else gain_
                        nc.scalar.activation(h_hi[:, k, :], halves(bk)[cc], ACT.Copy, scale=scale
                                             ).then_inc(hh_ready, 1)

            def hybrid():
                start_mixer()
                next_slab(0)
                next_slab(1)
                next_slab(2)
                for n, (to, k1) in enumerate(((0, 2), (2, 1))):
                    ready(n)
                    bk = bank()
                    read(nc.scalar.activation(vt[:, n, 0:2 * T], bk, ACT.Copy))
                    act.wait_ge(read_act, c["read_a"])
                    for k in range(k1):
                        nc.scalar.activation(hf[:, to + k, :], vt[:, n, k * T:(k + 1) * T], ACT.Square
                                             ).then_inc(sq_ready, 1)
                    if n == 0:
                        next_slab(0)
                c.take("sq", 3)
                next_slab(1)
                for k in range(2):
                    act.wait_ge(lat_u, k + 1)
                    nc.scalar.activation(g_hi[:, k * T:(k + 1) * T], gf[:, k * T:(k + 1) * T], ACT.Copy
                                         ).then_inc(lat_hi, 1)
                act.wait_ge(lat_u, 3)
                nc.scalar.activation(z_hi[:, 0:T], hf[:, 3, :], ACT.Copy).then_inc(lat_hi, 1)

                def copy_u(n, j):
                    ready(j)
                    if n >= 2:
                        act.wait_ge(cu_done, n - 1)
                    nc.scalar.activation(silu[:, (n % 2) * T:(n % 2 + 1) * T], bank()[:, 0:T], ACT.Copy
                                         ).then_inc(u_copied, 1)

                for n, j in enumerate((2, 3, 4)):
                    copy_u(n, j)
                    next_slab((j + 3) % 3)
                for h in range(0, 8, 2):
                    passing() if h < 6 else ready(5)
                    read(nc.scalar.activation(qT[0:64, h:h + 2, :].rearrange("p h t -> p (h t)"), bank()[0:64, :],
                                         ACT.Copy))
                next_slab(2)
                for h in range(0, 8, 2):
                    passing()
                    read(nc.scalar.activation(kT[0:64, h:h + 2, :].rearrange("p h t -> p (h t)"), bank()[0:64, :],
                                         ACT.Copy))
                c.take("passing")
                c.take("res", 2)
                next_slab(0)

                def w_out(slot):
                    return lambda: next_slab(slot)

                attention(mla_groups(), {0: lambda: copy_u(3, 7), 1: w_out(1), 2: w_out(2), 3: w_out(0)})
                c.take("res", 2)
                operand()
                act.wait_ge(yc_done, 2)
                ready(9)
                for k in range(4):
                    nc.scalar.activation(h_hi[:, k, :], hf[:, 4 + k, :], ACT.Copy).then_inc(hh_ready, 1)
                turn(4, first=4)
                next_slab(1)
                finish(10)

            def finish(j0):
                c["y_slot"] = ((j0 + 3) % 3, c[f"slot{(j0 + 3) % 3}"])

            def nsa():
                start_mixer()
                for j in range(3):
                    next_slab(j)
                for j in range(4):
                    ready(j)
                    read(nc.scalar.activation(qT[:, 2 * j:2 * j + 2, :].rearrange("p k t -> p (k t)"), bank(), ACT.Copy,
                                         scale=0.125))
                    next_slab(j % 3)
                for kv in range(2):
                    ready(4 + kv)
                    bk = bank()
                    th = (g_hi, z_hi)[kv]
                    b3, t3 = (a.rearrange("p (g t) -> p g t", g=2) for a in (bk, th[:, :]))
                    nc.scalar.activation(t3[0:64, :, 0:T - 1], b3[0:64, :, 0:T - 1], ACT.Copy)
                    nc.scalar.activation(t3[64:128, :, 0:T - 1], b3[64:128, :, 1:T], ACT.Copy).then_inc(cmp_hi, 1)
                    next_slab((4 + kv) % 3)
                act.wait_ge(kt_zeroed, 1)
                for n in range(2):
                    ready(6 + n)
                    bk = bank()
                    k3 = kT[:, 4 * n:4 * n + 4, :].rearrange("p (g m) t -> p g m t", g=2)
                    b3 = bk.rearrange("p (g t) -> p g t", g=2)
                    nc.scalar.activation(k3[0:64, :, 0, :], b3[0:64, :, :], ACT.Copy)
                    read(nc.scalar.activation(k3[64:128, :, 1, :], b3[64:128, :, :], ACT.Copy))
                    next_slab((6 + n) % 3)
                c.take("res", 2)
                act.wait_ge(gate_in, 1)
                nc.scalar.activation(gates[:, :, :], gates[:, :, :], ACT.Sigmoid).then_inc(gate_ready, 1)
                nc.scalar.activation(pe_hi[:, :], v("pe", 0, 64), ACT.Copy).then_inc(cmp_hi, 1)
                next_slab(11 % 3)
                for kv in range(2):
                    ready(10 + kv)
                    bk = bank()
                    link(nc.scalar.activation(hid_b[:, kv:kv + 1], bk[:, 2 * NCMP:2 * NCMP + 1], ACT.Copy))
                    nc.scalar.activation(hid[:, kv, :], bk[:, 0:2 * NCMP], ACT.Silu, bias=hid_b[:, kv:kv + 1]
                                         ).then_inc(hid_ready, 1)
                passing()
                bk = bank()
                nc.scalar.activation(kcz[0:64, 0, :], bk[0:64, 0:2 * NCMP], ACT.Copy)
                read(nc.scalar.activation(kcz[64:128, 1, :], bk[64:128, 0:2 * NCMP], ACT.Copy))
                passing()
                read(nc.scalar.activation(vcz[0:NCMP, :], bank()[0:NCMP, 0:128], ACT.Copy))
                for s in (0, 1, 2):
                    next_slab(s)
                attention(nsa_groups())
                operand()
                turn(8)
                next_slab(0)
                finish(12)

            def conformer():
                start_mixer()
                for j in range(3):
                    next_slab(j)
                for j in range(8):
                    ready(j)
                    if j >= 2:
                        act.wait_ge(cu_done, 4 + j - 1)
                    nc.scalar.activation(silu[:, (j % 2) * T:(j % 2 + 1) * T], bank()[:, T:2 * T], ACT.Sigmoid,
                                         bias=v("b_pw1", 8 + j)).then_inc(u_copied, 1)
                    next_slab(j % 3)
                s0 = c.take("sq", KD)
                for k in range(KD):
                    act.wait_ge(cen_ready, k + 1)
                    nc.scalar.activation(hf[:, k, :], qT[:, k, :], ACT.Square).then_inc(sq_ready, 1)
                operand()
                for k in range(KD + 1):
                    if k < KD:
                        act.wait_ge(ln_u, k + 1)
                        nc.scalar.activation(kT[:, k, :], hf[:, k, :], ACT.Silu, bias=v("ln_b", k)).then_inc(ln_silu, 1)
                    if k:
                        act.wait_ge(ln_silu, k)
                        nc.scalar.activation(h_hi[:, k - 1, :], kT[:, k - 1, :], ACT.Copy).then_inc(hh_ready, 1)
                next_slab(2)
                finish(8)

            def diff():
                start_mixer()
                for j in range(3):
                    next_slab(j)
                for j in range(4):
                    ready(j)
                    read(nc.scalar.activation(qT[:, 2 * j:2 * j + 2, :].rearrange("p k t -> p (k t)"), bank(), ACT.Copy,
                                         scale=0.125))
                    next_slab(j % 3)
                act.wait_ge(kt_zeroed, 2)
                for j in range(4, 8):
                    ready(j)
                    b3 = bank().rearrange("p (h t) -> p h t", h=2)
                    h = 2 * (j - 4)
                    nc.scalar.activation(kz[0:64, h:h + 2, 0, :], b3[0:64, :, :], ACT.Copy)
                    read(nc.scalar.activation(kz[64:128, h:h + 2, 1, :], b3[64:128, :, :], ACT.Copy))
                    next_slab(j % 3)
                for j in range(8, 12):
                    ready(j)
                    at = (j - 8) * 2 * P
                    read(nc.scalar.activation(vt[:, :, at:at + 2 * P], bank().rearrange("p (a b) -> p a b", a=TT), ACT.Copy))
                    next_slab(j % 3)
                passing()
                nc.scalar.activation(small[:, 6:8], bank()[:, 0:2], ACT.Exp, scale=float(P)).then_inc(lam_exp, 1)
                attention(diff_groups())
                operand()
                turn(8, gain_=gain[:, 0:1])
                next_slab(0)
                finish(12)

            steps = {"begin": begin, "norm": norm, "ffn": ffn, "add": add, "final": final, "hybrid": hybrid, "nsa": nsa,
                     "conformer": conformer, "diff": diff}
            for kind, *a in plan:
                if kind in steps:
                    steps[kind](*a)

        @block.vector
        def _(dve):
            c = Count()

            def link(ins):
                n = c.take("link") + 1
                ins.then_inc(dve_link, 1)
                dve.wait_ge(dve_link, n)

            def split(slot, n):
                dve.wait_ge(hi_done[slot], n + 1)
                nc.vector.tensor_tensor(lo[slot][:, :], raw[slot][:, :], hi[slot][:, :].bitcast(F32),
                                        ALU.subtract).then_inc(lo_done[slot], 1)

            def next_slab(slot):
                split(slot, c.take(f"slot{slot}"))

            def mac(buf, q, n):
                dve.wait_ge(ada_in_[buf], n * 16 + 16)
                w = ada_raw[:, buf, :].rearrange("p (k n) -> p k n", k=KD)
                nc.vector.tensor_scalar(ada_acc[:, :], w[:, 0, :], cact[:, 0:1], None, ALU.mult).then_inc(ada_mac, 1)
                for k in range(1, KD):
                    dve.wait_ge(ada_mac, q * KD + k)
                    nc.vector.scalar_tensor_tensor(ada_acc[:, :], w[:, k, :], cact[:, k:k + 1], ada_acc[:, :],
                                                   ALU.mult, ALU.add).then_inc(ada_mac, 1)

            def mod_out(q):
                dve.wait_ge(ada_cols, q + 1)
                at = q * PAIR
                b = vec[:, bass.ds(at + VEC["ada_b"][0], PAIR)]
                nc.vector.tensor_tensor(mod[:, bass.ds(at, PAIR)], M[:, 0:PAIR], b, ALU.add).then_inc(ada_mod, 1)

            def begin():
                nc.vector.memset(one[:, :], 1.0)
                for n, t in ones.items():
                    nc.vector.memset(t[:, :], 1.0 / n)
                nc.vector.memset(pr[:, :, :], 0.0)
                nc.vector.memset(small[:, :], 0.0)
                nc.vector.memset(zero_b[:, :], 0.0).then_inc(const_ready, 1)
                dve.wait_ge(act_ready, 1)
                for q in range(4):
                    mac(q % 2, q, q // 2)
                    mod_out(q)
                    if q == 0:
                        dve.wait_ge(con_loaded, 16)
                        con = hf[:, :, :].rearrange("p k t -> p (k t)")
                        nc.vector.tensor_copy(ident[:, :], con[:, 0:P])
                        nc.vector.tensor_copy(ident_b[:, :], con[:, 0:P])
                        nc.vector.tensor_copy(causal_b[:, :], con[:, CON["causal"]:CON["causal"] + P])
                        nc.vector.tensor_copy(dist_b[:, :, :].rearrange("p a b -> p (a b)"),
                                              con[:, CON["dist"]:CON["dist"] + TT * T])
                        nc.vector.tensor_copy(cmp_b[:, :, :].rearrange("p a b -> p (a b)"),
                                              con[:, CON["cmp"]:CON["cmp"] + TT * NCMP])
                        for h in range(8):
                            nc.vector.tensor_scalar(slope_b[:, h, :], con[:, 0:P], -SLOPES[h], None, ALU.mult)
                        nc.vector.tensor_copy(small[:, 0:4], con[:, CON["row_ok"]:CON["row_ok"] + 4]
                                              ).then_inc(const_ready, 1)
                        rope_angles()
                c["ada1"] = 2
                c["ada0"] = 2

            def rope_angles():
                pi = math.pi
                big = 1.5 * 2.0 ** 23
                c1 = 6.28125
                c2 = 2 * pi - c1
                ang, turns, cos_in = qT[:, 1, :], qT[:, 2, :], qT[:, 3, :]
                dve.wait_ge(pos_loaded, 16)
                dve.wait_ge(const_ready, 2)
                link(nc.vector.tensor_copy(ang, qT[:, 0, :].bitcast(I32)))
                link(nc.vector.tensor_scalar(ang, ang, small[:, 2:3], None, ALU.mult))
                link(nc.vector.tensor_scalar(turns, ang, 1 / (2 * pi), big, ALU.mult, ALU.add))
                link(nc.vector.tensor_scalar(turns, turns, -big, None, ALU.add))
                link(nc.vector.scalar_tensor_tensor(ang, turns, -c1, ang, ALU.mult, ALU.add))
                link(nc.vector.scalar_tensor_tensor(ang, turns, -c2, ang, ALU.mult, ALU.add))
                top = float(np.nextafter(np.float32(pi), np.float32(0)))
                link(nc.vector.tensor_scalar(ang, ang, top, -top, ALU.min, ALU.max))
                link(nc.vector.scalar_tensor_tensor(cos_in, ang, -1.0, ang, ALU.mult, ALU.max))
                nc.vector.tensor_scalar(cos_in, cos_in, -1.0, pi / 2, ALU.mult, ALU.add).then_inc(rope_in, 1)

            def rsqrt(y, value, t):
                link(nc.vector.tensor_scalar(y.bitcast(I32), value.bitcast(I32), -0.5, float(0x5f3759df),
                                             ALU.mult, ALU.add))
                for _ in range(3):
                    link(nc.vector.tensor_tensor(t, value, y, ALU.mult))
                    link(nc.vector.scalar_tensor_tensor(t, t, -0.5, y, ALU.mult, ALU.mult))
                    link(nc.vector.scalar_tensor_tensor(y, t, 1.5, y, ALU.add, ALU.mult))

            def rstd_of(eps, scale=None):
                dve.wait_ge(stat_ready, c.take("stat") + 1)
                link(nc.vector.tensor_scalar(var[:, :], N[:, 0:T], eps, None, ALU.add))
                rsqrt(rstd[:, :], var[:, :], gf[:, 0:T])
                if scale is not None:
                    link(nc.vector.tensor_scalar(rstd[:, :], rstd[:, :], scale, None, ALU.mult))

            def norm(n):
                if n < 6:
                    l, j = divmod(n, 3)
                    dve.wait_ge(ada_mod, c["mod"])
                    link(nc.vector.scalar_tensor_tensor(gain[:, :], modv(l, 3 * j + 1, 0, KD), 1.0,
                                                        v("norm_g", n * KD, KD), ALU.add, ALU.mult))
                    g = gain[:, :]
                else:
                    l, j = divmod(n - 6, 3)
                    g = v("mix_pre", l * KD, KD) if j == 1 else v("ffn_pre", (2 * l + j // 2) * KD, KD)
                rstd_of(EPS)
                u0 = c.take("u", KD)
                hh0 = c.take("hh", KD)
                c.take("h", KD)
                for k in range(KD + 1):
                    if k < KD:
                        nc.vector.scalar_tensor_tensor(hf[:, k, :], x[:, k, :], g[:, k:k + 1], rstd[:, :],
                                                       ALU.mult, ALU.mult).then_inc(u_ready, 1)
                    if k:
                        j = k - 1
                        dve.wait_ge(hh_ready, hh0 + k)
                        if n < 6:
                            ins = nc.vector.scalar_tensor_tensor(
                                h_lo[:, j, :], hf[:, j, :], modv(n // 3, 3 * (n % 3), j),
                                h_hi[:, j, :].bitcast(F32), ALU.add, ALU.subtract)
                        else:
                            ins = nc.vector.tensor_tensor(h_lo[:, j, :], hf[:, j, :], h_hi[:, j, :].bitcast(F32),
                                                          ALU.subtract)
                        ins.then_inc(h_ready, 1)

            def gate_mul(g, last_gf=True):
                dve.wait_ge(silu_done, g + 1)
                if last_gf:
                    dve.wait_ge(glo_done, g)
                nc.vector.tensor_tensor(gf[:, :], silu[:, :], AB[:, B, :], ALU.mult).then_inc(gf_done, 1)

            def gate_lo(g):
                dve.wait_ge(ghi_done, g + 1)
                nc.vector.tensor_tensor(g_lo[:, :], gf[:, :], g_hi[:, :].bitcast(F32), ALU.subtract
                                        ).then_inc(glo_done, 1)

            def ffn(f):
                q0, n_ada = ADA_FFN.get(f, (0, 0))
                a0 = c.take("ada0", n_ada)
                u = [c.take(f"slot{s}", NSTEP) for s in range(3)]
                g0 = c.take("g", NSTEP)
                split(A, u[A])
                split(B, u[B])
                if n_ada:
                    mac(0, q0, a0)

                def steps(lo_i, hi_i, out_, mac_):
                    with dve.Fori(lo_i, hi_i) as i:
                        split(A, i + u[A])
                        split(B, i + u[B])
                        gate_mul(i + (g0 - 1), last_gf=not mac_)
                        split(W, i + (u[W] - 1))
                        gate_lo(i + (g0 - 1))
                        if out_:
                            mod_out(i + (q0 - 1))
                        if mac_:
                            mac(0, i + q0, i + a0)

                if n_ada in (0, NSTEP):
                    steps(1, NSTEP, n_ada > 0, n_ada > 0)
                else:
                    steps(1, n_ada, True, True)
                    steps(n_ada, n_ada + 1, True, False)
                    steps(n_ada + 1, NSTEP, False, False)
                gate_mul(g0 + NSTEP - 1)
                split(W, u[W] + NSTEP - 1)
                gate_lo(g0 + NSTEP - 1)
                if n_ada == NSTEP:
                    mod_out(q0 + NSTEP - 1)
                if n_ada:
                    c["mod"] = q0 + n_ada
                c["y_slot"] = (W, u[W] + NSTEP)

            def add(n):
                c.take("x_new", KD)
                slot, value = c["y_slot"]
                half = 0.5 if n % 3 != 1 else 1.0
                if n < 6:
                    dve.wait_ge(ada_mod, c["mod"])
                    g_src = modv(n // 3, 3 * (n % 3) + 2, 0, KD)
                else:
                    l, j = divmod(n - 6, 3)
                    g_src = v("mix_post", l * KD, KD) if j == 1 else v("ffn_post", (2 * l + j // 2) * KD, KD)
                link(nc.vector.tensor_scalar(gate[:, :], g_src, half, None, ALU.mult))
                if n < 6:
                    dve.wait_ge(used[slot], value)
                    for k in range(KD):
                        nc.vector.scalar_tensor_tensor(x[:, k, :], Y[:, k, :], gate[:, k:k + 1], x[:, k, :],
                                                       ALU.mult, ALU.add).then_inc(x_new, 1)
                    return
                rstd_of(EPS)
                for k in range(KD + 1):
                    if k < KD:
                        bias = v("b_pw2", k) if n == 7 else 0.0
                        ins = nc.vector.scalar_tensor_tensor(hf[:, k, :], Y[:, k, :], bias, rstd[:, :],
                                                             ALU.add, ALU.mult)
                        ins.then_inc(dve_link, 1)
                        c.take("link")
                    if k:
                        dve.wait_ge(dve_link, c["link"] - (1 if k < KD else 0))
                        nc.vector.scalar_tensor_tensor(x[:, k - 1, :], hf[:, k - 1, :], gate[:, k - 1:k],
                                                       x[:, k - 1, :], ALU.mult, ALU.add).then_inc(x_new, 1)

            def final():
                c.take("x_new", KD)
                rstd_of(EPS)
                for k in range(KD):
                    nc.vector.scalar_tensor_tensor(x[:, k, :], x[:, k, :], v("final_g", k), rstd[:, :],
                                                   ALU.mult, ALU.mult).then_inc(x_new, 1)

            def start_mixer():
                c["base"] = [c.get(f"slot{s}", 0) for s in range(3)]

            def ready(j):
                dve.wait_ge(used[j % 3], c["base"][j % 3] + j // 3 + 1)

            def passing(n=1):
                dve.wait_ge(res_ready, c.take("passing", n) + n)

            def bank():
                return AB[:, c.take("res") % 2, :]

            def halves(bank_):
                return [bank_[:, 0:T], bank_[:, T:2 * T]]

            def reciprocals(bt, n):
                link(nc.vector.tensor_scalar(rec[:, 0:n], sums[:, bt % 2, 0:n], 1e-20, None, ALU.max))
                link(nc.vector.reciprocal(rec[:, 0:n], rec[:, 0:n]))

            def attention(groups, batch, beside=None):
                n = len(groups)
                g0 = c.take("grp", n)
                b0 = c.take("batch", groups[-1]["batch"] + 1)
                for s_ in range(n + 3):
                    if s_ < n:
                        G, gr = g0 + s_, groups[s_]
                        nu = len(gr["units"])
                        dve.wait_ge(s_ready, G + 1)
                        sc = score_bank(G).rearrange("p (u r) -> p u r", r=gr["room"])[:, 0:nu, 0:gr["nk"]]
                        nc.vector.tensor_reduce(nmax[:, G % 4, 0:nu], sc, AXX, ALU.max, negate=True
                                                ).then_inc(m_ready, 1)
                    if beside and s_ in beside:
                        beside[s_]()
                    if 1 <= s_ <= n:
                        G, gr = g0 + s_ - 1, groups[s_ - 1]
                        dve.wait_ge(t_ready, G + 1)
                        if G >= 2:
                            dve.wait_ge(pv_done, G - 1)
                        w = len(gr["units"]) * gr["tiles"] * P
                        nc.vector.tensor_copy(pT[:, G % 2, 0:w], turn_bank(G)[:, 0:w]).then_inc(pt_ready, 1)
                    if s_ >= 3:
                        g = s_ - 3
                        if g == n - 1 or groups[g + 1]["batch"] != groups[g]["batch"]:
                            dve.wait_ge(pv_done, g0 + g + 1)
                            bt = groups[g]["batch"]
                            batch(bt, b0 + bt)

            def turn(n_chunks, gain_=None, first=0):
                for m in range(n_chunks // 2):
                    bk = bank()
                    dve.wait_ge(hh_ready, c["hh"] - KD + first + 2 * m + 2)
                    for cc in range(2):
                        k = first + 2 * m + cc
                        if gain_ is None:
                            ins = nc.vector.tensor_tensor(h_lo[:, k, :], halves(bk)[cc], h_hi[:, k, :].bitcast(F32),
                                                          ALU.subtract)
                        else:
                            ins = nc.vector.scalar_tensor_tensor(h_lo[:, k, :], halves(bk)[cc], gain_,
                                                                 h_hi[:, k, :].bitcast(F32), ALU.mult, ALU.subtract)
                        ins.then_inc(h_ready, 1)

            def finish(j0):
                c["y_slot"] = ((j0 + 3) % 3, c[f"slot{(j0 + 3) % 3}"])

            def hybrid():
                start_mixer()
                q0, n_ada = ADA_MIX
                nc.vector.memset(cu[:, :, 0:2], 0.0)
                for s in (0, 1, 2, 0):
                    next_slab(s)
                c.take("res", 2)
                rstd_of(EPS, scale=float(96 ** -0.5))
                for k in range(2):
                    nc.vector.scalar_tensor_tensor(gf[:, k * T:(k + 1) * T], vt[:, 0, k * T:(k + 1) * T],
                                                   v("q_norm", k), rstd[:, :], ALU.mult, ALU.mult).then_inc(lat_u, 1)
                dve.wait_ge(lat_hi, 2)
                nc.vector.tensor_tensor(g_lo[:, :], gf[:, :], g_hi[:, :].bitcast(F32), ALU.subtract
                                        ).then_inc(lat_ready, 1)
                rstd_of(EPS)
                nc.vector.scalar_tensor_tensor(hf[:, 3, :], vt[:, 1, 0:T], v("kv_norm"), rstd[:, :], ALU.mult,
                                               ALU.mult).then_inc(lat_u, 1)
                dve.wait_ge(rope_ready, 1)
                kr = vt[:, 1, T:2 * T]
                nc.vector.tensor_tensor(gf[64:96, 0:T], kr[96:128, :], sin_[96:128, :], ALU.mult)
                link(nc.vector.tensor_tensor(hf[64:96, 1, :], kr[64:96, :], cos_[64:96, :], ALU.mult))
                link(nc.vector.tensor_tensor(hf[64:96, 1, :], hf[64:96, 1, :], gf[64:96, 0:T], ALU.add))
                nc.vector.tensor_copy(kT[64:96, :, :], hf[64:96, 1, :].unsqueeze(1).to_broadcast([32, 8, T]))
                dve.wait_ge(lat_hi, 3)
                nc.vector.tensor_tensor(z_lo[:, 0:T], hf[:, 3, :], z_hi[:, 0:T].bitcast(F32), ALU.subtract
                                        ).then_inc(lat_ready, 1)
                next_slab(1)

                def conv(n):
                    dve.wait_ge(u_copied, c.take("cu") + 1)
                    nc.vector.tensor_tensor(cu[:, n, 2:T + 2], silu[:, (n % 2) * T:(n % 2 + 1) * T], bank()[:, T:2 * T],
                                            ALU.mult).then_inc(cu_done, 1)
                    dve.wait_ge(cu_done, c["cu"])
                    y = hf[:, 4 + n, :]
                    link(nc.vector.tensor_scalar(y, cu[:, n, 0:T], v("hy_conv", n), None, ALU.mult))
                    for tap in (1, 2):
                        link(nc.vector.scalar_tensor_tensor(y, cu[:, n, tap:tap + T], v("hy_conv", tap * 4 + n), y,
                                                            ALU.mult, ALU.add))

                for n in range(3):
                    conv(n)
                    next_slab((n + 5) % 3)
                for q in range(q0, q0 + n_ada):
                    mac(0, q, c.take("ada0"))
                    mod_out(q)
                c["mod"] = q0 + n_ada
                dve.wait_ge(rope_ready, 1)
                s2, c2 = (a.unsqueeze(1).to_broadcast([32, 2, T]) for a in (sin_[96:128, :], cos_[64:96, :]))
                for h in range(0, 8, 2):
                    passing() if h < 6 else ready(5)
                    bk = bank().rearrange("p (h t) -> p h t", h=2)
                    g3 = gf[64:96, :].rearrange("p (h t) -> p h t", h=2)
                    nc.vector.tensor_tensor(g3, bk[96:128, :, :], s2, ALU.mult)
                    nc.vector.tensor_tensor(qT[64:96, h:h + 2, :], bk[64:96, :, :], c2, ALU.mult
                                            ).then_inc(read_dve, 1)
                    dve.wait_ge(read_dve, c.take("read_d") + 1)
                    link(nc.vector.tensor_tensor(qT[64:96, h:h + 2, :], qT[64:96, h:h + 2, :], g3, ALU.add))
                next_slab(2)
                c.take("passing", 4)
                c.take("res", 4)
                for t in range(TT):
                    passing() if t == 0 else ready(6)
                    nc.vector.tensor_copy(vt[:, t, 0:512], bank()).then_inc(read_dve, 1)
                    c.take("read_d")
                next_slab(0)

                def batch(t, bt):
                    reciprocals(bt, 8)
                    nc.vector.tensor_tensor(ot[:, t, 0:512].rearrange("p (h n) -> p h n", h=8),
                                            out_bank(bt)[:, :].rearrange("p (h n) -> p h n", h=8),
                                            rec[:, 0:8].unsqueeze(2).to_broadcast([P, 8, 64]), ALU.mult
                                            ).then_inc(o_read, 1)

                def gate_b(m, j):
                    def run():
                        ready(j)
                        y = hf[:, 4 + 2 * m:6 + 2 * m, :].rearrange("p k t -> p (k t)")
                        nc.vector.tensor_tensor(y, bank(), y, ALU.mult).then_inc(yc_done, 1)
                        next_slab((j + 2) % 3)
                    return run

                def last():
                    next_slab(0)

                attention(mla_groups(), batch, {0: lambda: conv(3), 1: gate_b(0, 8), 2: gate_b(1, 9), 3: last})
                hh0 = c.take("hh", KD)
                c.take("h", KD)
                for k in range(4):
                    dve.wait_ge(hh_ready, hh0 + k + 1)
                    nc.vector.tensor_tensor(h_lo[:, k, :], hf[:, 4 + k, :], h_hi[:, k, :].bitcast(F32), ALU.subtract
                                            ).then_inc(h_ready, 1)
                turn(4, first=4)
                next_slab(1)
                finish(10)

            def nsa():
                start_mixer()
                kt3 = kT[:, :, :].rearrange("p (g m) t -> p g m t", m=2)
                nc.vector.memset(kt3[0:64, :, 1, :], 0.0)
                nc.vector.memset(kt3[64:128, :, 0, :], 0.0).then_inc(kt_zeroed, 1)
                for s in (0, 1, 2, 0, 1, 2, 0):
                    next_slab(s)
                c.take("res", 4)
                for kv in range(2):
                    bk = bank()
                    th, tl = ((g_hi, g_lo), (z_hi, z_lo))[kv]
                    b3, h3, l3 = (a.rearrange("p (g t) -> p g t", g=2) for a in (bk, th[:, :], tl[:, :]))
                    dve.wait_ge(cmp_hi, kv + 1)
                    nc.vector.tensor_tensor(l3[0:64, :, 0:T - 1], b3[0:64, :, 0:T - 1],
                                            h3[0:64, :, 0:T - 1].bitcast(F32), ALU.subtract)
                    nc.vector.tensor_tensor(l3[64:128, :, 0:T - 1], b3[64:128, :, 1:T],
                                            h3[64:128, :, 0:T - 1].bitcast(F32), ALU.subtract).then_inc(cmp_in, 1)
                    next_slab((4 + kv) % 3)
                for j in (6, 7):
                    next_slab(j % 3)
                c.take("res", 2)
                ready(8)
                nc.vector.tensor_copy(vt[:, :, 0:2 * P], bank().rearrange("p (a b) -> p a b", a=TT)
                                      ).then_inc(read_dve, 1)
                c.take("read_d")
                ready(9)
                nc.vector.tensor_tensor(gates[:, :, :], bank()[:, 0:96].rearrange("p (a b) -> p a b", a=TT),
                                        v("gate_b", 0, 48).unsqueeze(1).to_broadcast([P, TT, 48]), ALU.add
                                        ).then_inc(gate_in, 1)
                dve.wait_ge(cmp_hi, 3)
                nc.vector.tensor_tensor(pe_lo[:, :], v("pe", 0, 64), pe_hi[:, :].bitcast(F32), ALU.subtract
                                        ).then_inc(cmp_in, 1)
                next_slab(11 % 3)
                c.take("res", 4)
                c.take("passing", 2)
                for s in (0, 1, 2):
                    next_slab(s)
                dve.wait_ge(gate_ready, 1)

                def batch(b_, bt):
                    t, rest = divmod(b_, 6)
                    g, branch = divmod(rest, 3)
                    reciprocals(bt, 8)
                    gs = gates[:, t, :].rearrange("p (h b) -> p h b", b=3)[:, 8 * g:8 * g + 8, branch]
                    if branch == 0:
                        link(nc.vector.scalar_tensor_tensor(rec[:, 0:8], rec[:, 0:8], small[:, t:t + 1], gs,
                                                            ALU.mult, ALU.mult))
                    else:
                        link(nc.vector.tensor_tensor(rec[:, 0:8], rec[:, 0:8], gs, ALU.mult))
                    o = ot[:, t, g * 512:(g + 1) * 512]
                    to = o if branch == 0 else gf[:, :]
                    ins = nc.vector.tensor_tensor(to.rearrange("p (h n) -> p h n", h=8),
                                                  out_bank(bt)[:, :].rearrange("p (h n) -> p h n", h=8),
                                                  rec[:, 0:8].unsqueeze(2).to_broadcast([P, 8, 64]), ALU.mult)
                    if branch:
                        link(ins)
                        ins = nc.vector.tensor_tensor(o, o, gf[:, :], ALU.add)
                    ins.then_inc(o_read, 1)
                    dve.wait_ge(o_read, bt + 1)

                attention(nsa_groups(), batch)
                c.take("hh", KD)
                c.take("h", KD)
                turn(8)
                next_slab(0)
                finish(12)

            def conformer():
                start_mixer()
                nc.vector.memset(upad[:, :, 0:15], 0.0)
                nc.vector.memset(upad[:, :, 15 + T:30 + T], 0.0)
                for s in (0, 1, 2):
                    next_slab(s)

                def taps(j):
                    for tap in range(31):
                        for k in (j, j + 1):
                            src = upad[:, k, tap:tap + T]
                            n = c.take("link") if tap < 30 else c["link"]
                            if tap == 0:
                                ins = nc.vector.tensor_scalar(qT[:, k, :], src, v("w_dw", k), v("b_dw", k), ALU.mult,
                                                              ALU.add)
                            else:
                                dve.wait_ge(dve_link, n - 1 if tap < 30 else c["link"] - 1 + (k - j))
                                ins = nc.vector.scalar_tensor_tensor(qT[:, k, :], src, v("w_dw", tap * KD + k),
                                                                     qT[:, k, :], ALU.mult, ALU.add)
                            ins.then_inc(dve_link if tap < 30 else dw_done, 1)

                for j in range(8):
                    dve.wait_ge(u_copied, c.take("cu") + 1)
                    nc.vector.scalar_tensor_tensor(upad[:, j, 15:15 + T], bank()[:, 0:T], v("b_pw1", j),
                                                   silu[:, (j % 2) * T:(j % 2 + 1) * T], ALU.add, ALU.mult
                                                   ).then_inc(cu_done, 1)
                    next_slab(j % 3)
                    if j % 2:
                        dve.wait_ge(cu_done, c["cu"])
                        taps(j - 1)
                dve.wait_ge(mean_ready, 1)
                link(nc.vector.tensor_copy(rstd[:, :], N[:, 0:T]))
                for k in range(KD):
                    nc.vector.tensor_tensor(qT[:, k, :], qT[:, k, :], rstd[:, :], ALU.subtract).then_inc(cen_ready, 1)
                rstd_of(1e-5)
                hh0 = c.take("hh", KD)
                c.take("h", KD)
                for k in range(KD):
                    nc.vector.scalar_tensor_tensor(hf[:, k, :], qT[:, k, :], v("ln_g", k), rstd[:, :], ALU.mult,
                                                   ALU.mult).then_inc(ln_u, 1)
                for k in range(KD):
                    dve.wait_ge(hh_ready, hh0 + k + 1)
                    nc.vector.tensor_tensor(h_lo[:, k, :], kT[:, k, :], h_hi[:, k, :].bitcast(F32), ALU.subtract
                                            ).then_inc(h_ready, 1)
                next_slab(2)
                finish(8)

            def diff():
                start_mixer()
                nc.vector.memset(kz[0:64, :, 1, :], 0.0)
                nc.vector.memset(kz[64:128, :, 0, :], 0.0).then_inc(kt_zeroed, 1)
                nc.vector.tensor_tensor(small[:, 4:6], v("lam", 0, 2), v("lam", 2, 2), ALU.mult).then_inc(lam_in, 1)
                link(nc.vector.tensor_scalar(gain[:, 0:1], v("subln"), 1.0 - LAMBDA_INIT, None, ALU.mult))
                for j in range(15):
                    next_slab(j % 3)
                c.take("res", 13)
                dve.wait_ge(lam_exp, 1)
                c.take("passing")
                link(nc.vector.tensor_scalar(small[:, 204:205], small[:, 7:8], small[:, 6:7], -LAMBDA_INIT,
                                             ALU.subtract, ALU.add))

                def batch(b_, bt):
                    t, hp = divmod(b_, 4)
                    reciprocals(bt, 4)
                    link(nc.vector.tensor_scalar(rec[:, 1:4:2], rec[:, 1:4:2], small[:, 204:205], None, ALU.mult))
                    g4 = gf[:, :].rearrange("p (h n) -> p h n", h=4)
                    link(nc.vector.tensor_tensor(g4, out_bank(bt)[:, :].rearrange("p (h n) -> p h n", h=4),
                                                 rec[:, 0:4].unsqueeze(2).to_broadcast([P, 4, P]), ALU.mult))
                    nc.vector.tensor_tensor(ot[:, t, hp * 2 * P:(hp + 1) * 2 * P].rearrange("p (h n) -> p h n", h=2),
                                            g4[:, 0:4:2, :], g4[:, 1:4:2, :], ALU.add).then_inc(o_read, 1)
                    dve.wait_ge(o_read, bt + 1)

                attention(diff_groups(), batch)
                for t in range(TT):
                    sq = hf[:, 4 * t:4 * t + 4, :].rearrange("p k t -> p (k t)")
                    o = ot[:, t, :]
                    link(nc.vector.tensor_tensor(sq, o, o, ALU.mult))
                    link(nc.vector.tensor_reduce(rec[:, 0:8], sq.rearrange("p (h n) -> p h n", h=8), AXX, ALU.add))
                    link(nc.vector.tensor_scalar(var[:, 0:8], rec[:, 0:8], 1.0 / P, 1e-5, ALU.mult, ALU.add))
                    rsqrt(rec[:, 0:8], var[:, 0:8], gf[:, 0:8])
                    nc.vector.tensor_tensor(o.rearrange("p (h n) -> p h n", h=8), o.rearrange("p (h n) -> p h n", h=8),
                                            rec[:, 0:8].unsqueeze(2).to_broadcast([P, 8, P]), ALU.mult
                                            ).then_inc(ot_ready, 1)
                c.take("hh", KD)
                c.take("h", KD)
                turn(8, gain_=gain[:, 0:1])
                next_slab(0)
                finish(12)

            c["mod"] = 4
            steps = {"begin": begin, "norm": norm, "ffn": ffn, "add": add, "final": final, "hybrid": hybrid, "nsa": nsa,
                     "conformer": conformer, "diff": diff}
            for kind, *a in plan:
                if kind in steps:
                    steps[kind](*a)


def chunks_(a):
    a = np.ascontiguousarray(a).reshape(-1, P)
    return a.T


def slab_of(*cols):
    a = np.concatenate(cols, axis=1)
    if a.shape[1] < 2 * P:
        a = np.concatenate([a, np.zeros((D, 2 * P - a.shape[1]), a.dtype)], axis=1)
    return a.reshape(KD, P, 2 * P).transpose(1, 0, 2).reshape(P, SLAB)


def rows_slab(a):
    return a.reshape(2, P, D).transpose(1, 0, 2).reshape(P, SLAB)


def ffn_slabs(a, b, w):
    for i in range(NSTEP + 1):
        if i < NSTEP:
            yield slab_of(a[:, i * STEP:(i + 1) * STEP])
            yield slab_of(b[:, i * STEP:(i + 1) * STEP])
        if i:
            yield rows_slab(w[(i - 1) * STEP:i * STEP])


def wide(w):
    for j in range(w.shape[1] // (2 * P)):
        yield slab_of(w[:, j * 2 * P:(j + 1) * 2 * P])


def twice(a):
    return np.concatenate([a, a], axis=1)


def all_slabs(i):
    for layer in range(2):
        for half in range(2):
            w13 = i["ff_w13"][layer, half]
            if half:
                if layer == 0:
                    w = i["hy_w_in"][0]
                    u, gc, gb = w[:, 0:512], w[:, 512:1024], w[:, 1024:1536]
                    cq, ckv, kr = w[:, 1536:1792], w[:, 1792:1920], w[:, 1920:1952]
                    yield slab_of(cq)
                    yield slab_of(ckv, np.zeros((D, 64), w.dtype), kr, kr[:, 16:32], kr[:, 0:16])
                    for j in range(3):
                        yield slab_of(u[:, j * P:(j + 1) * P], gc[:, j * P:(j + 1) * P])
                    uq = i["hy_w_uq"][0].reshape(2, P, 8, 96)
                    uq = np.concatenate([uq, uq[..., 80:96], uq[..., 64:80]], axis=3)
                    yield uq.transpose(1, 0, 2, 3).reshape(P, SLAB)
                    yield np.concatenate([i["hy_w_ukv"][0], np.zeros((P, D), w.dtype)], axis=1)
                    yield slab_of(u[:, 3 * P:4 * P], gc[:, 3 * P:4 * P])
                    yield slab_of(gb[:, 0:2 * P])
                    yield slab_of(gb[:, 2 * P:4 * P])
                    yield from wide(i["hy_w_out"][0])
                else:
                    w = i["nsa_w_in"][0]
                    yield from wide(w[:, 0:1024])
                    kc, vc, ks, vs, kw, vw = (w[:, 1024 + n * P:1024 + (n + 1) * P] for n in range(6))
                    for a in (kc, vc, ks, kw):
                        yield slab_of(twice(a[:, 0:64]), twice(a[:, 64:128]))
                    yield slab_of(vs, vw)
                    yield slab_of(w[:, 1792:1840])
                    for kv in range(2):
                        yield i["nsa_cmp_w1"][0, kv].reshape(16, P, P).transpose(1, 0, 2).reshape(P, SLAB)
                    yield from wide(i["nsa_w_out"][0])
            yield from ffn_slabs(w13[:, 0:FF], w13[:, FF:], i["ff_w2"][layer, half])
    for layer in range(2):
        for half in range(2):
            if half:
                if layer == 0:
                    w = i["conv_w_pw1_2"][0]
                    for j in range(KD):
                        yield slab_of(w[:, j * P:(j + 1) * P], w[:, D + j * P:D + (j + 1) * P])
                    yield from wide(i["conv_w_pw2_2"][0])
                else:
                    yield from wide(i["attn_w_qkv_2"][0])
                    yield from wide(i["attn_w_o_2"][0])
            yield from ffn_slabs(i["ffn_w_gate_2"][layer, half], i["ffn_w_up_2"][layer, half],
                                 i["ffn_w_down_2"][layer, half])


def vectors(i):
    def rows(a):
        return np.concatenate([a, np.zeros((P - a.shape[0], a.shape[1]), a.dtype)], axis=0)

    pe = np.repeat(i["nsa_cmp_pe"][0].reshape(2, 16, P).reshape(32, P), 2, axis=0).T
    lam = rows(np.stack([i[f"attn_lambda_{n}_2"][0] for n in ("q1", "q2", "k1", "k2")], axis=1))
    parts = {
        "c": chunks_(i["c"]), "ada_b": chunks_(i["ada_b"]), "norm_g": chunks_(i["norm_g"]),
        "final_g": chunks_(i["final_g"]), "hy_conv": chunks_(i["hy_conv_w"]), "q_norm": chunks_(i["hy_q_norm"]),
        "kv_norm": chunks_(i["hy_kv_norm"]), "pe": pe, "ffn_pre": chunks_(i["ffn_norm_pre_2"]),
        "ffn_post": chunks_(i["ffn_norm_post_2"]), "mix_pre": chunks_(i["mix_norm_pre_2"]),
        "mix_post": chunks_(i["mix_norm_post_2"]), "b_pw1": chunks_(i["conv_b_pw1_2"]),
        "w_dw": chunks_(i["conv_w_dw_2"]), "b_dw": chunks_(i["conv_b_dw_2"]), "ln_g": chunks_(i["conv_ln_g_2"]),
        "ln_b": chunks_(i["conv_ln_b_2"]), "b_pw2": chunks_(i["conv_b_pw2_2"]), "subln": chunks_(i["attn_subln_g_2"]),
        "lam": lam, "gate_b": np.broadcast_to(i["nsa_gate_b"], (P, 48)),
        "cmp_w2k": twice(i["nsa_cmp_w2"][0, 0]), "cmp_w2v": i["nsa_cmp_w2"][0, 1],
    }
    for name, (_, n) in VEC.items():
        assert parts[name].shape == (P, n), name
    return np.concatenate([parts[name] for name in VEC], axis=1)


def layout(inputs):
    i = {k: np.asarray(a) for k, a in inputs.items()}
    ada = i["ada_w"].reshape(2, KD, P, NPAIR // 2, PAIR * P).transpose(0, 3, 2, 1, 4).reshape(NPAIR, P, 2 * SLAB)
    return {
        "x_t": np.ascontiguousarray(i["x"][0].T.reshape(KD, P, T).transpose(1, 0, 2)),
        "positions": i["positions"],
        "vectors": np.ascontiguousarray(vectors(i)),
        "constants": constants(),
        "ada": np.ascontiguousarray(ada),
        "slabs": np.stack(list(all_slabs(i))),
    }


def kernel(**inputs):
    import concourse.bacc as _bacc
    from concourse.bass_utils import run_bass_kernel_spmd as _run

    nc = _bacc.Bacc("TRN2", target_bir_lowering=False, num_devices=1)
    arrays = layout(inputs)
    args = [nc.dram_tensor(name, a.shape, mybir.dt.from_np(a.dtype), kind="ExternalInput").ap()
            for name, a in arrays.items()]
    out = nc.dram_tensor("out_t", (P, KD, T), F32, kind="ExternalOutput").ap()
    program(nc, *args, out)
    r = _run(nc, [arrays], core_ids=[0])
    return r.results[0]["out_t"].transpose(2, 1, 0).reshape(1, T, D)
```

```python
import math
from contextlib import ExitStack
from itertools import groupby

import numpy as np

import concourse.bass as bass
from concourse import mybir

F32 = mybir.dt.float32
F32R = mybir.dt.float32r
BF16 = mybir.dt.bfloat16
I32 = mybir.dt.int32
ALU = mybir.AluOpType
ACT = mybir.ActivationFunctionType
AXX = mybir.AxisListType.X

P = 128
T = 256
TT = T // P
D = 1024
KD = D // P
FF = 2816
STEP = 2 * P
NSTEP = FF // STEP
SLAB = 2048
EPS = 1e-6
DVE_TAPS = 20
NADA = 9
PAIR = 4
NPAIR = 2 * NADA * KD // PAIR
NEG = -1e30

LAMBDA_INIT = 0.8 - 0.6 * math.exp(-0.3)

A, B = 0, 1


def inv_freq():
    half = 16
    return (np.float32(10000.0) ** (-np.arange(half, dtype=np.float32) / np.float32(half))).astype(np.float32)


VEC = {}


def _columns():
    at = 0
    for name, n in (
        ("c", 8), ("ada_b", 144), ("norm_g", 48), ("final_g", 8), ("hy_conv", 12), ("q_norm", 2), ("kv_norm", 1),
        ("pe", 64), ("ffn_pre", 32), ("ffn_post", 32), ("mix_pre", 16), ("mix_post", 16), ("b_pw1", 16),
        ("w_dw", 248), ("b_dw", 8), ("ln_g", 8), ("ln_b", 8), ("b_pw2", 8), ("subln", 1), ("lam", 4),
        ("gate_b", 48), ("cmp_w2k", 128), ("cmp_w2v", 64),
    ):
        VEC[name] = (at, n)
        at += n
    return at


NVEC = _columns()

CON = {"ident": 0, "causal": 128, "dist": 256, "cmp": 768, "row_ok": 798, "inv": 800, "sign": 801}
NCON = 802
NCMP = (T - 32) // 16 + 1
SLOPES = [2.0 ** (-8.0 * (h + 1.0) / 8) for h in range(8)]


def constants():
    c = np.zeros((P, NCON), np.float32)
    r = np.arange(P)
    c[:, 0:128] = np.eye(P)
    c[:, 128:256] = np.where(r[None, :] <= r[:, None], 0.0, NEG)
    for t in range(TT):
        q = t * P + r
        c[:, 256 + t * T:256 + (t + 1) * T] = np.abs(q[:, None] - np.arange(T)[None, :])
        end = np.arange(NCMP) * 16 + 31
        c[:, 768 + t * NCMP:768 + (t + 1) * NCMP] = np.where(end[None, :] <= q[:, None], 0.0, NEG)
        c[:, 798 + t] = q >= 31
    c[:, 800] = inv_freq()[r % 16]
    c[:, 801] = np.where(r % 32 < 16, -1.0, 1.0)
    return c


class Count(dict):

    def take(self, name, n=1):
        v = self.get(name, 0)
        self[name] = v + n
        return v


def program(nc, x_in, pos_in, vec_in, con_in, ada_in, stream_in, out):
    ctx = ExitStack()
    with ctx:
        def sb(name, shape, dt=F32):
            return ctx.enter_context(nc.sbuf_tensor(name, shape, dt))

        def ps(name, shape):
            return ctx.enter_context(nc.psum_tensor(name, shape, F32))

        def sem(name):
            return ctx.enter_context(nc.semaphore(name))

        raw = [sb(f"raw{s}", [P, SLAB]) for s in range(3)]
        hi = [sb(f"hi{s}", [P, SLAB], F32R) for s in range(3)]
        lo = [sb(f"lo{s}", [P, SLAB], F32R) for s in range(3)]
        ada_raw = sb("ada_raw", [P, 2, 2 * SLAB])
        ada_acc = sb("ada_acc", [P, PAIR * P])
        x = sb("x", [P, KD, T])
        hf = sb("hf", [P, KD, T])
        h_hi = sb("h_hi", [P, KD, T], F32R)
        h_lo = sb("h_lo", [P, KD, T], F32R)
        silu = sb("silu", [P, 2 * T])
        gf = sb("gf", [P, 2 * T])
        g_hi = sb("g_hi", [P, 2 * T], F32R)
        g_lo = sb("g_lo", [P, 2 * T], F32R)
        z_hi = sb("z_hi", [P, 2 * T], F32R)
        z_lo = sb("z_lo", [P, 2 * T], F32R)
        rstd = sb("rstd", [P, T])
        root = sb("root", [P, TT])
        var = sb("var", [P, 8])
        vec = sb("vec", [P, NVEC])
        cact = sb("cact", [P, 8])
        mod = sb("mod", [P, 2 * NADA * KD])
        gain = sb("gain", [P, KD])
        gate = sb("gate", [P, KD])
        ident = sb("ident", [P, P])
        ones = {n: sb(f"ones{n}", [P, P]) for n in (1024, 256, 128)}
        one = sb("one", [P, 2])
        ident_b = sb("ident_b", [P, P], BF16)
        causal_b = sb("causal_b", [P, P], BF16)
        dist_b = sb("dist_b", [P, TT, T], BF16)
        cmp_b = sb("cmp_b", [P, TT, NCMP], BF16)
        slope_b = sb("slope_b", [P, 8, P], BF16)
        zero_b = sb("zero_b", [P, 512], BF16)
        small = sb("small", [P, 208])
        hid = sb("hid", [P, 2, 2 * NCMP])
        qT = sb("qT", [P, KD, T])
        kT = sb("kT", [P, KD, T])
        vt = sb("vt", [P, TT, D])
        ot = sb("ot", [P, TT, D])
        pr = sb("pr", [P, 3, 2 * T])
        pT = sb("pT", [P, 2, 2 * T])
        nmax = sb("nmax", [P, 4, 4])
        sums = sb("sums", [P, 3, 8])
        rec = sb("rec", [P, 8])
        gates = sb("gates", [P, TT, 48])

        Y = ps("Y", [P, KD, T])
        AB = ps("AB", [P, 2, 512])
        M = ps("M", [P, 512])
        N = ps("N", [P, 512])

        x_loaded = sem("x_loaded")
        vec_loaded = sem("vec_loaded")
        con_loaded = sem("con_loaded")
        pos_loaded = sem("pos_loaded")
        raw_in = [sem(f"raw_in{s}") for s in range(3)]
        hi_done = [sem(f"hi_done{s}") for s in range(3)]
        lo_done = [sem(f"lo_done{s}") for s in range(3)]
        used = [sem(f"used{s}") for s in range(3)]
        ada_in_ = [sem(f"ada_in{s}") for s in range(3)]
        ada_mac = sem("ada_mac")
        ada_cols = sem("ada_cols")
        ada_mod = sem("ada_mod")
        act_ready = sem("act_ready")
        const_ready = sem("const_ready")
        x_new = sem("x_new")
        sq_ready = sem("sq_ready")
        pair_ready = sem("pair_ready")
        y_ready = sem("y_ready")
        stat_ready = sem("stat_ready")
        root_ready = sem("root_ready")
        rstd_ready = sem("rstd_ready")
        u_ready = sem("u_ready")
        hh_ready = sem("hh_ready")
        h_ready = sem("h_ready")
        silu_done = sem("silu_done")
        gf_done = sem("gf_done")
        ghi_done = sem("ghi_done")
        glo_done = sem("glo_done")
        dve_link = sem("dve_link")
        act_link = sem("act_link")
        stored = sem("stored")
        rope_in = sem("rope_in")
        rope_ready = sem("rope_ready")
        res_ready = sem("res_ready")
        read_act = sem("read_act")
        read_dve = sem("read_dve")
        u_copied = sem("u_copied")
        cu_done = sem("cu_done")
        yc_done = sem("yc_done")
        lat_u = sem("lat_u")
        lat_hi = sem("lat_hi")
        lat_ready = sem("lat_ready")
        s_ready = sem("s_ready")
        m_ready = sem("m_ready")
        p_ready = sem("p_ready")
        t_ready = sem("t_ready")
        pt_ready = sem("pt_ready")
        pv_done = sem("pv_done")
        o_read = sem("o_read")
        ot_ready = sem("ot_ready")
        turned = sem("turned")
        cmp_copied = sem("cmp_copied")
        blk_ready = sem("blk_ready")
        cmp_hi = sem("cmp_hi")
        cmp_in = sem("cmp_in")
        hid_ready = sem("hid_ready")
        kt_zeroed = sem("kt_zeroed")
        gate_in = sem("gate_in")
        gate_ready = sem("gate_ready")
        diag_ready = sem("diag_ready")
        dw_part = sem("dw_part")
        dw_done = sem("dw_done")
        mean_ready = sem("mean_ready")
        cen_ready = sem("cen_ready")
        ln_u = sem("ln_u")
        ln_silu = sem("ln_silu")
        lam_in = sem("lam_in")
        lam_exp = sem("lam_exp")

        def v(name, i=0, n=1, rows=slice(None)):
            at = VEC[name][0] + i
            return vec[rows, at:at + n]

        def modv(layer, j, k=0, n=1):
            at = (layer * NADA + j) * KD + k
            return mod[:, at:at + n]

        def mm3(out_, w_hi, w_lo, r_hi, r_lo, start, stop, **kw):
            nc.tensor.matmul(out_, w_hi, r_hi, start=start, stop=False, **kw)
            nc.tensor.matmul(out_, w_hi, r_lo, start=False, stop=False, **kw)
            return nc.tensor.matmul(out_, w_lo, r_hi, start=False, stop=stop, **kw)

        block = ctx.enter_context(nc.Block())

        plan = [("begin",)]
        for n in range(6):
            layer, j = divmod(n, 3)
            plan.append(("norm", n))
            plan.append([("ffn", 2 * layer + j // 2), ("hybrid",) if layer == 0 else ("nsa",)][j == 1])
            plan.append(("add", n))
        plan.append(("final",))
        for n in range(6):
            layer, j = divmod(n, 3)
            plan.append(("norm", 6 + n))
            plan.append([("ffn", 4 + 2 * layer + j // 2), ("conformer",) if layer == 0 else ("diff",)][j == 1])
            plan.append(("add", 6 + n))
        plan.append(("end",))
        NSLAB = sum({"ffn": 3 * NSTEP, "hybrid": 14, "nsa": 16, "conformer": 12, "diff": 16}.get(kind, 0)
                    for kind, *_ in plan)

        ADA_FFN = {0: (4, 10), 1: (16, 10), 2: (26, 8), 3: (34, 2)}
        ADA_MIX = (14, 15)
        LEAD = {"mla": 1, "nsa": 2, "diff": 2}

        def score_bank(g, lead):
            b = g % (lead + 1)
            return Y[:, 2 * b:2 * b + 2, :].rearrange("p k t -> p (k t)") if b < 2 else AB[:, 0, :]

        def turn_bank(G):
            return Y[:, 4 + 2 * (G % 2):6 + 2 * (G % 2), :].rearrange("p k t -> p (k t)")

        def out_bank(bt):
            return M if bt % 2 == 0 else N

        cu = ada_raw[:, 1, 0:4 * (T + 2)].rearrange("p (k t) -> p k t", k=4)
        kz = ada_raw[:, 0, :].rearrange("p (h m t) -> p h m t", h=8, m=2)
        upad = ada_raw[:, 0, 0:KD * (T + 30)].rearrange("p (k t) -> p k t", k=KD)
        cos_, sin_ = ot[:, 1, 512:768], ot[:, 1, 768:1024]
        blocks = [hf[:, 2 * kv:2 * kv + 2, :].rearrange("p k t -> p (k t)")[:, 0:32 * NCMP] for kv in range(2)]
        kcz = small[:, 8:8 + 4 * NCMP].rearrange("p (m n) -> p m n", m=2)
        vcz = small[:, 72:72 + 2 * 64]

        TAPS = 31
        taps_dve = [DVE_TAPS] * (KD - 2) + [15, 15]
        diag = [a.rearrange("p t (n m) -> p (t n) m", m=P) for a in (vt, ot)]

        def mla_groups():
            gs = []
            for t in range(TT):
                for h in range(0, 8, 2):
                    nk = (t + 1) * P
                    gs.append(dict(
                        units=[(qT[0:96, h + u, t * P:(t + 1) * P], kT[0:96, h + u, 0:nk],
                                [(t * P, ident_b[:, :], causal_b[:, :])]) for u in range(2)],
                        nk=nk, room=T, tiles=t + 1, batch=t, scale=1.0, sums=h,
                        pv=[((h + u) * 64, [vt[:, j, (h + u) * 64:(h + u + 1) * 64] for j in range(t + 1)])
                            for u in range(2)]))
            return gs

        def nsa_groups():
            gs, bt = [], 0
            for t in range(TT):
                for g in range(2):
                    for branch in range(3):
                        if branch == 0:
                            for h in range(0, 8, 4):
                                us = []
                                for u in range(4):
                                    head = g * 8 + h + u
                                    us.append((qT[:, head // 2, t * P:(t + 1) * P],
                                               kcz[:, head % 2, g:g + 2 * (NCMP - 1) + 1:2],
                                               [(0, ident_b[:, :], cmp_b[:, t, :])]))
                                gs.append(dict(units=us, nk=NCMP, room=P, tiles=1, batch=bt, sums=h,
                                               pv=[((h + u) * 64, [vcz[0:NCMP, g * 64:(g + 1) * 64]])
                                                   for u in range(4)]))
                        else:
                            nk = (t + 1) * P
                            for h in range(0, 8, 2):
                                us = []
                                for u in range(2):
                                    head = g * 8 + h + u
                                    us.append((qT[:, head // 2, t * P:(t + 1) * P],
                                               kT[:, 4 * (branch - 1) + 2 * g + head % 2, 0:nk],
                                               [(t * P, ident_b[:, :], causal_b[:, :])]))
                                at = (branch - 1) * P + g * 64
                                gs.append(dict(units=us, nk=nk, room=T, tiles=t + 1, batch=bt, sums=h,
                                               pv=[((h + u) * 64, [vt[:, j, at:at + 64] for j in range(t + 1)])
                                                   for u in range(2)]))
                        bt += 1
            return gs

        def diff_groups():
            gs = []
            for t in range(TT):
                for h in range(8):
                    gs.append(dict(
                        units=[(qT[:, h, t * P:(t + 1) * P], kz[:, h, m, :],
                                [(0, slope_b[:, h, :], dist_b[:, t, :])]) for m in range(2)],
                        nk=T, room=T, tiles=TT, batch=t * 4 + h // 2, sums=(h % 2) * 2,
                        pv=[(((h % 2) * 2 + m) * P, [vt[:, j, h * P:(h + 1) * P] for j in range(TT)])
                            for m in range(2)]))
            return gs


        def step_slots(j):
            return [((j + r) % 3, (j + r) // 3 - 1) for r in range(3)]

        def result_bank(eng, c, n, b):
            last = c["slab"] - c["ahead"] - 1
            if n % 3 == 1:
                j = last - 3 + b
                eng.wait_ge(used[j % 3], j // 3 + 1)
            elif b < 3:
                eng.wait_ge(y_ready, 3 * (n // 3 * 2 + n % 3 // 2) + b + 1)
            else:
                eng.wait_ge(used[last % 3], last // 3 + 1)

        @block.sync
        def _(sp):
            c = Count()

            def load(slot, slab, n):
                if not isinstance(n, int) or n:
                    sp.wait_ge(lo_done[slot], n)
                sp.dma_start(raw[slot][:, :], stream_in[bass.ds(slab, 1), :, :].rearrange("a p n -> (a p) n")
                             ).then_inc(raw_in[slot], 16)

            def next_slab():
                j = c.take("slab")
                load(j % 3, j, j // 3)

            def load_ada(buf, q, done):
                if done is not None:
                    sp.wait_ge(ada_mac, done)
                sp.dma_start(ada_raw[:, buf, :], ada_in[bass.ds(q, 1), :, :].rearrange("a p n -> (a p) n")
                             ).then_inc(ada_in_[buf], 16)

            def begin():
                sp.dma_start(vec[:, :], vec_in).then_inc(vec_loaded, 16)
                load_ada(0, 0, None)
                sp.dma_start(x[:, :, :], x_in).then_inc(x_loaded, 16)
                load_ada(1, 1, None)
                sp.dma_start(hf[:, :, :].rearrange("p k t -> p (k t)")[:, 0:NCON], con_in).then_inc(con_loaded, 16)
                sp.dma_start(qT[:, 0, :].bitcast(I32), pos_in.partition_broadcast(P)).then_inc(pos_loaded, 16)
                for n, to in enumerate((kT[:, :, :].rearrange("p k t -> p (k t)"),
                                        vt[:, :, :].rearrange("p a b -> p (a b)"))):
                    sp.dma_start(to, ada_in[2, :, n * SLAB:(n + 1) * SLAB]).then_inc(ada_in_[2], 16)
                load_ada(0, 3, KD)

            def ffn(f):
                q0, n_ada = ADA_FFN.get(f, (0, 0))
                next_slab()
                next_slab()
                if n_ada:
                    load_ada(0, q0, KD * q0)
                next_slab()
                j0 = c.take("slab", 3 * NSTEP - 3) - 1
                (sa, na), (sb_, nb), (sw, nw) = step_slots(j0)

                def step(i, ada, a):
                    load(sb_, i * 3 + (j0 - 2), i + nb)
                    load(sw, i * 3 + (j0 - 1), i + nw)
                    if a:
                        load(sa, i * 3 + j0, i + (na + 1))
                    if ada:
                        load_ada(0, i + q0, i * KD + KD * q0)

                for flags, run in groupby(range(1, NSTEP), lambda i: (i < n_ada, i < NSTEP - 1)):
                    run = list(run)
                    with sp.Fori(run[0], run[-1] + 1) as i:
                        step(i, *flags)
                c["slab"] -= 1
                next_slab()

            def mixer(n):
                for _ in range(n):
                    next_slab()

            def hybrid():
                mixer(3)
                load_ada(0, ADA_MIX[0], KD * ADA_MIX[0])
                mixer(2)
                load_ada(0, ADA_MIX[1], KD * ADA_MIX[1])
                mixer(5)
                mixer(4)

            def end():
                sp.wait_ge(x_new, c["x_new"])
                sp.dma_start(out, x[:, :, :]).then_inc(stored, 16)
                sp.wait_ge(stored, 16)

            steps = {"begin": begin, "ffn": ffn, "hybrid": hybrid, "nsa": lambda: mixer(16),
                     "conformer": lambda: mixer(12), "diff": lambda: mixer(16), "end": end,
                     "add": lambda n: c.take("x_new", KD), "final": lambda: c.take("x_new", KD)}
            for kind, *a in plan:
                if kind in steps:
                    steps[kind](*a)

        @block.tensor
        def _(pe):
            c = Count()

            def slab():
                j = c.take("slab")
                pe.wait_ge(lo_done[j % 3], j // 3 + 1)
                return hi[j % 3], lo[j % 3], used[j % 3]

            def cols(q):
                pe.wait_ge(ada_mac, q * KD + KD)
                for j in range(PAIR):
                    mm = nc.tensor.matmul(M[:, j:j + 1], ada_acc[:, j * P:(j + 1) * P], one[:, 0:1],
                                          start=True, stop=True)
                mm.then_inc(ada_cols, 1)

            def begin():
                pe.wait_ge(const_ready, 1)
                cols(0)
                stat_pairs()
                for q in range(1, 4):
                    cols(q)

            def stat(n_chunks, ones_, base=0, done=sq_ready, every=1):
                s0 = c.take("pair" if done is pair_ready else "sq", n_chunks)
                for k in range(n_chunks):
                    pe.wait_ge(done, s0 + k + 1)
                    for t in range(TT):
                        mm = nc.tensor.matmul((M, N)[t][:, 0:1], hf[:, base + every * k, t * P:(t + 1) * P], ones_[:, 0:1],
                                              start=(k == 0), stop=(k == n_chunks - 1))
                mm.then_inc(stat_ready, 1)
                pe.wait_ge(root_ready, c.take("stat") + 1)
                for t in range(TT):
                    mm = nc.tensor.matmul(N[:, t * P:(t + 1) * P], root[:, t:t + 1].to_broadcast([P, P]),
                                          ident[:, :], start=True, stop=True)
                mm.then_inc(rstd_ready, 1)

            def stat_pairs():
                c.take("sq", KD)
                stat(KD // 2, ones[1024], done=pair_ready, every=2)

            def norm(n):
                if n:
                    stat_pairs()
                c.take("h", KD)

            def wait_h(k):
                pe.wait_ge(h_ready, c["h"] - KD + k + 1)

            def up(first, ab, slot):
                for cc in range(2):
                    for k in range(KD):
                        if first and cc == 0:
                            wait_h(k)
                        at = k * 2 * P + cc * P
                        mm = mm3(AB[:, ab, cc * T:(cc + 1) * T], hi[slot][:, at:at + P], lo[slot][:, at:at + P],
                                 h_hi[:, k, :], h_lo[:, k, :], k == 0, k == KD - 1)
                mm.then_inc(used[slot], 1)

            def down(slot, t_hi=g_hi, t_lo=g_lo, last=False):
                for n in range(KD):
                    for cc in range(2):
                        at = cc * D + n * P
                        mm = mm3(Y[:, n, :], hi[slot][:, at:at + P], lo[slot][:, at:at + P],
                                 t_hi[:, cc * T:(cc + 1) * T], t_lo[:, cc * T:(cc + 1) * T], False, False,
                                 skip_group_check=True)
                    if last and n % 2 and n < KD - 1:
                        mm.then_inc(y_ready, 1)
                mm.then_inc(used[slot], 1)

            def ffn(f):
                q0, n_ada = ADA_FFN.get(f, (0, 0))
                g0 = c.take("g", NSTEP)
                for ab in range(2):
                    j = c.take("slab")
                    pe.wait_ge(lo_done[j % 3], j // 3 + 1)
                    up(ab == 0, ab, j % 3)
                for b in range(4):
                    nc.tensor.matmul(Y[:, 2 * b:2 * b + 2, :].rearrange("p k t -> p (k t)"), zero_b[:, 0:P],
                                     zero_b[:, :], start=True, stop=False, skip_group_check=True)

                ring = step_slots(c.take("slab", 3 * NSTEP - 3))

                def steps(lo_i, hi_i, ada):
                    with pe.Fori(lo_i, hi_i) as i:
                        if ada:
                            cols(i + (q0 - 1))
                        pe.wait_ge(lo_done[ring[0][0]], i + (ring[0][1] + 1))
                        pe.wait_ge(gf_done, i + g0)
                        up(False, 0, ring[0][0])
                        pe.wait_ge(lo_done[ring[1][0]], i + (ring[1][1] + 1))
                        up(False, 1, ring[1][0])
                        pe.wait_ge(lo_done[ring[2][0]], i + (ring[2][1] + 1))
                        pe.wait_ge(glo_done, i + g0)
                        down(ring[2][0])

                for ada, run in groupby(range(1, NSTEP), lambda i: i <= n_ada):
                    run = list(run)
                    steps(run[0], run[-1] + 1, ada)
                if n_ada == NSTEP:
                    cols(q0 + NSTEP - 1)
                j = c.take("slab")
                pe.wait_ge(lo_done[j % 3], j // 3 + 1)
                pe.wait_ge(glo_done, g0 + NSTEP)
                down(j % 3, z_hi, z_lo, last=True)

            def add(n):
                if n >= 6:
                    stat_pairs()

            def final():
                stat_pairs()

            READERS = {"a": read_act, "d": read_dve, "c": cu_done, "y": yc_done, "h": hid_ready, "m": cmp_copied,
                       "g": gate_in, "e": lam_exp}

            def result(*readers):
                o = c.take("res")
                old = c.setdefault("hist", [])
                if o >= 2:
                    for s_, n_ in old[o - 2]:
                        pe.wait_ge(s_, n_)
                old.append([r if isinstance(r, tuple) else (READERS[r], c.take("read_" + r) + 1) for r in readers])
                return AB[:, o % 2, :]

            def halves(bank):
                return [bank[:, 0:T], bank[:, T:2 * T]]

            def all_read():
                pe.wait_ge(read_act, c["read_a"])
                pe.wait_ge(read_dve, c["read_d"])

            def features(outs, first=False):
                w_hi, w_lo, done = slab()
                for cc in range(2):
                    for k in range(KD):
                        if first and cc == 0:
                            wait_h(k)
                        at = k * 2 * P + cc * P
                        mm = mm3(outs[cc], w_hi[:, at:at + P], w_lo[:, at:at + P], h_hi[:, k, :], h_lo[:, k, :],
                                 k == 0, k == KD - 1)
                return mm.then_inc(done, 1)

            def tokens(outs, n):
                w_hi, w_lo, done = slab()
                for t in range(TT):
                    for k in range(KD):
                        mm = mm3(outs[t], h_hi[:, k, t * P:(t + 1) * P], h_lo[:, k, t * P:(t + 1) * P],
                                 w_hi[:, k * 2 * P:k * 2 * P + n], w_lo[:, k * 2 * P:k * 2 * P + n],
                                 k == 0, k == KD - 1)
                return mm.then_inc(done, 1)

            def out_product():
                c.take("h", KD)
                for j in range(4):
                    features([Y[:, 2 * j, :], Y[:, 2 * j + 1, :]], first=(j == 0))

            def turn(n_chunks):
                for m in range(n_chunks // 2):
                    bank = result((h_ready, c["h"] + KD - n_chunks + 2 * m + 2))
                    for cc in range(2):
                        for t in range(TT):
                            at = (2 * m + cc) * P
                            mm = nc.tensor.transpose(bank[:, cc * T + t * P:cc * T + (t + 1) * P],
                                                     ot[:, t, at:at + P], ident[:, :])
                    mm.then_inc(turned, 1)

            def attention(groups, lead, beside=None):
                g0 = c.take("grp", len(groups))
                b0 = c.take("batch", groups[-1]["batch"] + 1)

                def scores(g):
                    G, gr = g0 + g, groups[g]
                    if g > lead:
                        pe.wait_ge(p_ready, G - lead)
                    for u, (q_ap, k_ap, bias) in enumerate(gr["units"]):
                        out_ = score_bank(g, lead)[:, u * gr["room"]:u * gr["room"] + gr["nk"]]
                        nc.tensor.matmul(out_, q_ap, k_ap, start=True, stop=not bias)
                        for i, (b_at, l_ap, r_ap) in enumerate(bias):
                            mm = nc.tensor.matmul(out_[:, b_at:b_at + r_ap.shape[-1]], l_ap, r_ap, start=False,
                                                  stop=(i == len(bias) - 1))
                    mm.then_inc(s_ready, 1)

                def transposes(g):
                    G, gr = g0 + g, groups[g]
                    pe.wait_ge(p_ready, G + 1)
                    if G >= 2:
                        pe.wait_ge(pt_ready, G - 1)
                    n = 0
                    for u in range(len(gr["units"])):
                        for t in range(gr["tiles"]):
                            at = u * gr["room"] + t * P
                            mm = nc.tensor.transpose(turn_bank(G)[:, n * P:(n + 1) * P], pr[:, G % 3, at:at + P],
                                                     ident[:, :])
                            n += 1
                    mm.then_inc(t_ready, 1)

                def values(g):
                    G, gr = g0 + g, groups[g]
                    pe.wait_ge(pt_ready, G + 1)
                    bt = b0 + gr["batch"]
                    if bt >= 2:
                        pe.wait_ge(o_read, bt - 1)
                    n = 0
                    for out_at, vs in gr["pv"]:
                        out_ = out_bank(bt)[:, out_at:out_at + vs[0].shape[-1]]
                        for t, v_ap in enumerate(vs):
                            rows_ = v_ap.shape[0]
                            mm = nc.tensor.matmul(out_, pT[0:rows_, G % 2, n * P:(n + 1) * P], v_ap, start=(t == 0),
                                                  stop=(t == len(vs) - 1))
                            n += 1
                    mm.then_inc(pv_done, 1)

                for s_ in range(len(groups) + lead + 1):
                    if s_ < len(groups):
                        scores(s_)
                    if beside and s_ in beside:
                        beside[s_]()
                    if lead <= s_ < len(groups) + lead:
                        transposes(s_ - lead)
                    if s_ > lead:
                        values(s_ - lead - 1)

            def hybrid():
                features(halves(result("a")), first=True)
                features(halves(result("a")))
                cols(ADA_MIX[0])
                features(halves(result("c")))
                pe.wait_ge(ada_mod, ADA_MIX[0] + 1)
                stat(2, ones[256])
                pe.wait_ge(lat_u, 1)
                stat(1, ones[128], 2)
                features(halves(result("c")))
                features(halves(result("c")))
                cols(ADA_MIX[1])
                w_hi, w_lo, done = slab()
                pe.wait_ge(lat_ready, 2)
                for h in range(0, 8, 2):
                    outs = halves(result("a", "d"))
                    for cc in range(2):
                        for r in range(2):
                            at = r * D + (h + cc) * P
                            mm = mm3(outs[cc], w_hi[:, at:at + P], w_lo[:, at:at + P], g_hi[:, r * T:(r + 1) * T],
                                     g_lo[:, r * T:(r + 1) * T], r == 0, r == 1)
                    mm.then_inc(res_ready if h < 6 else done, 1)
                w_hi, w_lo, done = slab()
                for h in range(0, 8, 2):
                    outs = halves(result("a"))
                    for cc in range(2):
                        at = (h + cc) * P
                        mm = mm3(outs[cc], w_hi[:, at:at + P], w_lo[:, at:at + P], z_hi[:, 0:T], z_lo[:, 0:T],
                                 True, True)
                    mm.then_inc(res_ready, 1)
                for t in range(TT):
                    bank = result("d")
                    vh, vl = (s_[:, 0:8 * P].rearrange("p (h n) -> p h n", h=8)[:, :, 64:128] for s_ in (w_hi, w_lo))
                    mm = mm3(bank, z_hi[:, t * P:(t + 1) * P], z_lo[:, t * P:(t + 1) * P], vh, vl, True, True)
                    mm.then_inc(res_ready if t == 0 else done, 1)
                all_read()

                def conv_slab(reader):
                    return lambda: features(halves(result(reader)))

                attention(mla_groups(), LEAD["mla"], {0: conv_slab("c"), 1: conv_slab("y"), 2: conv_slab("y")})
                pe.wait_ge(o_read, c["batch"])
                turn(4)
                out_product()

            def nsa():
                for j in range(4):
                    features(halves(result("a")), first=(j == 0))
                for j in (4, 5):
                    features(halves(result("m")))
                for j in (6, 7):
                    features(halves(result("a")))
                tokens(halves(result("d")), 2 * P)
                bank = result("g")
                tokens([bank[:, 0:48], bank[:, 48:96]], 48)
                for kv in range(2):
                    w_hi, w_lo, done = slab()
                    pe.wait_ge(cmp_in, kv + 1)
                    bank = result("h")
                    th, tl = ((g_hi, g_lo), (z_hi, z_lo))[kv]
                    for j in range(16):
                        mm = mm3(bank[:, 0:2 * NCMP], w_hi[:, j * P:(j + 1) * P], w_lo[:, j * P:(j + 1) * P],
                                 th[:, j * 2 * NCMP:(j + 1) * 2 * NCMP], tl[:, j * 2 * NCMP:(j + 1) * 2 * NCMP],
                                 j == 0, j == 15)
                    mm.then_inc(done, 1)
                pe.wait_ge(hid_ready, 2)
                bank = result("a")
                nc.tensor.matmul(bank[:, 0:2 * NCMP], v("cmp_w2k", 0, 128), hid[:, 0, :], start=True, stop=True
                                 ).then_inc(res_ready, 1)
                bank = result("a")
                for g in range(2):
                    mm = nc.tensor.matmul(bank[0:NCMP, g * 64:(g + 1) * 64],
                                          hid[:, 1, :].rearrange("p (n g) -> p g n", g=2)[:, g, :],
                                          v("cmp_w2v", 0, 64), start=True, stop=True)
                mm.then_inc(res_ready, 1)
                all_read()
                attention(nsa_groups(), LEAD["nsa"])
                pe.wait_ge(o_read, c["batch"])
                turn(8)
                out_product()

            def conformer():
                def taps(k):
                    pe.wait_ge(diag_ready, k + 1)
                    pe.wait_ge(cu_done, 4 + k + 1)
                    for tap in range(taps_dve[k], TAPS):
                        mm = nc.tensor.matmul(Y[:, k, :], diag[k % 2][:, tap - taps_dve[k], :],
                                              upad[:, k, tap:tap + T], start=(tap == taps_dve[k]),
                                              stop=(tap == TAPS - 1))
                    mm.then_inc(dw_part, 1)

                for j in range(8):
                    features(halves(result("c")), first=(j == 0))
                    if j >= 2:
                        taps(j - 2)
                taps(6)
                taps(7)
                for k in range(KD):
                    pe.wait_ge(dw_done, k + 1)
                    mm = nc.tensor.matmul(N[:, 0:T], ones[1024][:, :], qT[:, k, :], start=(k == 0), stop=(k == KD - 1))
                mm.then_inc(mean_ready, 1)
                stat_pairs()
                out_product()

            def diff():
                for j in range(8):
                    features(halves(result("a")), first=(j == 0))
                for j in range(8, 12):
                    tokens(halves(result("a")), 2 * P)
                pe.wait_ge(lam_in, 1)
                bank = result("e")
                nc.tensor.matmul(bank[:, 0:2], ones[128][:, :], small[:, 4:6], start=True, stop=True
                                 ).then_inc(res_ready, 1)
                all_read()
                pe.wait_ge(lam_exp, 1)
                attention(diff_groups(), LEAD["diff"])
                pe.wait_ge(ot_ready, TT)
                turn(8)
                out_product()

            steps = {"begin": begin, "norm": norm, "ffn": ffn, "add": add, "final": final, "hybrid": hybrid, "nsa": nsa,
                     "conformer": conformer, "diff": diff}
            for kind, *a in plan:
                if kind in steps:
                    steps[kind](*a)

        @block.gpsimd
        def _(pool):
            c = Count()

            def pairs():
                s0 = c.take("sq", KD)
                for k in range(0, KD, 2):
                    pool.wait_ge(sq_ready, s0 + k + 2)
                    nc.gpsimd.tensor_tensor(hf[:, k, :], hf[:, k, :], hf[:, k + 1, :], ALU.add
                                            ).then_inc(pair_ready, 1)

            def diagonals():
                for k in range(KD):
                    if k >= 2:
                        pool.wait_ge(dw_part, k - 1)
                    n = TAPS - taps_dve[k]
                    w = v("w_dw", taps_dve[k] * KD, n * KD).rearrange("p (t k) -> p t k", k=KD)[:, :, k]
                    nc.gpsimd.tensor_tensor(diag[k % 2][:, 0:n, :], ident[:, :].unsqueeze(1).to_broadcast([P, n, P]),
                                            w.unsqueeze(2).to_broadcast([P, n, P]), ALU.mult
                                            ).then_inc(diag_ready, 1)

            for kind, *a in plan:
                if kind == "conformer":
                    diagonals()
                if kind in ("norm", "final", "conformer") or kind == "add" and a[0] >= 6:
                    pairs()
                elif kind == "hybrid":
                    c.take("sq", 3)

        @block.scalar
        def _(act):
            c = Count()

            def link(ins):
                act_n = c.take("link") + 1
                ins.then_inc(act_link, 1)
                act.wait_ge(act_link, act_n)

            def split(slot, n):
                if not isinstance(n, int) or n:
                    act.wait_ge(used[slot], n)
                act.wait_ge(raw_in[slot], n * 16 + 16)
                nc.scalar.activation(hi[slot][:, :], raw[slot][:, :], ACT.Copy).then_inc(hi_done[slot], 1)

            def next_slab():
                if c.get("ahead", 0):
                    c["ahead"] -= 1
                else:
                    j = c.take("slab")
                    split(j % 3, j // 3)

            def ahead(n=2):
                n = min(n, NSLAB - c.get("slab", 0))
                for _ in range(n):
                    next_slab()
                c["ahead"] = n

            def begin():
                act.wait_ge(vec_loaded, 16)
                nc.scalar.activation(cact[:, :], v("c", 0, 8), ACT.Silu).then_inc(act_ready, 1)
                act.wait_ge(x_loaded, 16)
                act.wait_ge(const_ready, 2)
                squares()
                ahead(1)

            def squares():
                for k in range(KD):
                    if c.get("x_new"):
                        act.wait_ge(x_new, c["x_new"] - KD + k + 1)
                    nc.scalar.activation(hf[:, k, :], x[:, k, :], ACT.Square).then_inc(sq_ready, 1)

            def rope_tables():
                act.wait_ge(rope_in, 1)
                nc.scalar.activation(sin_, qT[:, 1, :], ACT.Sin, scale=small[:, 3:4])
                nc.scalar.activation(cos_, qT[:, 3, :], ACT.Sin).then_inc(rope_ready, 1)

            def norm(n):
                u0 = c.take("u", KD)
                c.take("hh", KD)
                if n:
                    squares()
                for k in range(KD):
                    act.wait_ge(u_ready, u0 + k + 1)
                    if n < 6:
                        nc.scalar.activation(h_hi[:, k, :], hf[:, k, :], ACT.Identity,
                                             bias=modv(n // 3, 3 * (n % 3), k)).then_inc(hh_ready, 1)
                    else:
                        nc.scalar.activation(h_hi[:, k, :], hf[:, k, :], ACT.Copy).then_inc(hh_ready, 1)

            def g_split(g, to=g_hi):
                act.wait_ge(gf_done, g + 1)
                nc.scalar.activation(to[:, :], gf[:, :], ACT.Copy).then_inc(ghi_done, 1)

            def ffn(f):
                g0 = c.take("g", NSTEP)
                next_slab()
                next_slab()
                next_slab()
                if f == 0:
                    rope_tables()
                j0 = c.take("slab", 3 * NSTEP - 4) - 1
                (sa, na), (sb_, nb), (sw, nw) = step_slots(j0)

                def step(i, slot_b, n_b, a=True):
                    act.wait_ge(used[slot_b], n_b)
                    nc.scalar.activation(silu[:, :], AB[:, A, :], ACT.Silu).then_inc(silu_done, 1)
                    split(sb_, i + nb)
                    split(sw, i + nw)
                    g_split(i + (g0 - 1))
                    if a:
                        split(sa, i + (na + 1))

                step(1, (j0 - 1) % 3, (j0 - 1) // 3 + 1)
                with act.Fori(2, NSTEP - 1) as i:
                    step(i, sb_, i + nb)
                step(NSTEP - 1, sb_, NSTEP - 1 + nb, a=False)
                j = c["slab"] - 2
                act.wait_ge(used[j % 3], j // 3 + 1)
                nc.scalar.activation(silu[:, :], AB[:, A, :], ACT.Silu).then_inc(silu_done, 1)
                next_slab()
                g_split(g0 + NSTEP - 1, z_hi)
                ahead()

            def add(n):
                c.take("x_new", KD)
                if n >= 6:
                    for k in range(KD):
                        if k % 2 == 0:
                            result_bank(act, c, n, k // 2)
                        bias = v("b_pw2", k) if n == 7 else 0.0
                        nc.scalar.activation(hf[:, k, :], Y[:, k, :], ACT.Square, bias=bias).then_inc(sq_ready, 1)

            def final():
                for k in range(KD):
                    act.wait_ge(x_new, c["x_new"] - KD + k + 1)
                    nc.scalar.activation(hf[:, k, :], x[:, k, :], ACT.Square).then_inc(sq_ready, 1)
                c.take("x_new", KD)

            def start_mixer():
                c["base"] = c["slab"] - c["ahead"]

            def ready(j):
                j += c["base"]
                act.wait_ge(used[j % 3], j // 3 + 1)

            def passing(n=1):
                act.wait_ge(res_ready, c.take("passing", n) + n)

            def halves(bank):
                return [bank[:, 0:T], bank[:, T:2 * T]]

            def bank():
                return AB[:, c.take("res") % 2, :]

            def read(ins):
                c.take("read_a")
                ins.then_inc(read_act, 1)

            def operand():
                return c.take("hh", KD)

            def attention(groups, lead, beside=None):
                g0 = c.take("grp", len(groups))
                b0 = c.take("batch", groups[-1]["batch"] + 1)
                for s_, gr in enumerate(groups):
                    G, bt = g0 + s_, b0 + gr["batch"]
                    act.wait_ge(m_ready, G + 1)
                    if G >= 3:
                        act.wait_ge(t_ready, G - 2)
                    if gr["sums"] == 0 and bt >= 3:
                        act.wait_ge(o_read, bt - 2)
                    for u in range(len(gr["units"])):
                        at = u * gr["room"]
                        ins = nc.scalar.activation(
                            pr[:, G % 3, at:at + gr["nk"]], score_bank(s_, lead)[:, at:at + gr["nk"]], ACT.Exp,
                            bias=nmax[:, G % 4, u:u + 1], accum_out=sums[:, bt % 3, gr["sums"] + u:gr["sums"] + u + 1])
                    ins.then_inc(p_ready, 1)
                    if beside and s_ in beside:
                        beside[s_]()

            def turn(n_chunks, gain_=None, first=0):
                for m in range(n_chunks // 2):
                    bk = bank()
                    act.wait_ge(turned, c.take("turned") + 1)
                    for cc in range(2):
                        k = first + 2 * m + cc
                        scale = 1.0 if gain_ is None else gain_
                        nc.scalar.activation(h_hi[:, k, :], halves(bk)[cc], ACT.Copy, scale=scale
                                             ).then_inc(hh_ready, 1)

            def hybrid():
                start_mixer()
                next_slab()
                next_slab()
                next_slab()
                for n, (to, k1) in enumerate(((0, 2), (2, 1))):
                    ready(n)
                    bk = bank()
                    read(nc.scalar.activation(vt[:, n, 0:2 * T], bk, ACT.Copy))
                    act.wait_ge(read_act, c["read_a"])
                    for k in range(k1):
                        nc.scalar.activation(hf[:, to + k, :], vt[:, n, k * T:(k + 1) * T], ACT.Square
                                             ).then_inc(sq_ready, 1)
                    if n == 0:
                        next_slab()
                next_slab()
                for k in range(2):
                    act.wait_ge(lat_u, k + 1)
                    nc.scalar.activation(g_hi[:, k * T:(k + 1) * T], gf[:, k * T:(k + 1) * T], ACT.Copy
                                         ).then_inc(lat_hi, 1)
                act.wait_ge(lat_u, 3)
                nc.scalar.activation(z_hi[:, 0:T], hf[:, 3, :], ACT.Copy).then_inc(lat_hi, 1)

                def copy_u(n, j):
                    ready(j)
                    if n >= 2:
                        act.wait_ge(cu_done, n - 1)
                    nc.scalar.activation(silu[:, (n % 2) * T:(n % 2 + 1) * T], bank()[:, 0:T], ACT.Copy
                                         ).then_inc(u_copied, 1)

                for n, j in enumerate((2, 3, 4)):
                    copy_u(n, j)
                    next_slab()
                for h in range(0, 8, 2):
                    passing() if h < 6 else ready(5)
                    read(nc.scalar.activation(qT[0:64, h:h + 2, :].rearrange("p h t -> p (h t)"), bank()[0:64, :],
                                         ACT.Copy))
                next_slab()
                for h in range(0, 8, 2):
                    passing()
                    read(nc.scalar.activation(kT[0:64, h:h + 2, :].rearrange("p h t -> p (h t)"), bank()[0:64, :],
                                         ACT.Copy))
                c.take("passing")
                c.take("res", 2)
                next_slab()

                attention(mla_groups(), LEAD["mla"], {0: lambda: copy_u(3, 7), 1: next_slab, 2: next_slab, 3: next_slab})
                c.take("res", 2)
                operand()
                act.wait_ge(yc_done, 2)
                ready(9)
                for k in range(4):
                    nc.scalar.activation(h_hi[:, k, :], hf[:, 4 + k, :], ACT.Copy).then_inc(hh_ready, 1)
                turn(4, first=4)
                next_slab()
                ahead()

            def nsa():
                start_mixer()
                for _ in range(3):
                    next_slab()
                for j in range(4):
                    ready(j)
                    read(nc.scalar.activation(qT[:, 2 * j:2 * j + 2, :].rearrange("p k t -> p (k t)"), bank(), ACT.Copy,
                                         scale=0.125))
                    next_slab()
                for kv in range(2):
                    ready(4 + kv)
                    bk = bank()
                    to = (silu, gf)[kv]
                    b3, t3 = (a.rearrange("p (g t) -> p g t", g=2) for a in (bk, to[:, :]))
                    nc.scalar.activation(t3[0:64, :, :], b3[0:64, :, :], ACT.Copy)
                    nc.scalar.activation(t3[64:128, :, 0:T - 1], b3[64:128, :, 1:T], ACT.Copy
                                         ).then_inc(cmp_copied, 1)
                    next_slab()
                act.wait_ge(kt_zeroed, 1)
                for n in range(2):
                    ready(6 + n)
                    bk = bank()
                    k3 = kT[:, 4 * n:4 * n + 4, :].rearrange("p (g m) t -> p g m t", g=2)
                    b3 = bk.rearrange("p (g t) -> p g t", g=2)
                    nc.scalar.activation(k3[0:64, :, 0, :], b3[0:64, :, :], ACT.Copy)
                    read(nc.scalar.activation(k3[64:128, :, 1, :], b3[64:128, :, :], ACT.Copy))
                    next_slab()
                c.take("res", 2)
                act.wait_ge(gate_in, 1)
                nc.scalar.activation(gates[:, :, :], gates[:, :, :], ACT.Sigmoid).then_inc(gate_ready, 1)
                for kv in range(2):
                    act.wait_ge(blk_ready, kv + 1)
                    nc.scalar.activation((g_hi, z_hi)[kv][:, 0:32 * NCMP], blocks[kv], ACT.Copy).then_inc(cmp_hi, 1)
                next_slab()
                for kv in range(2):
                    ready(10 + kv)
                    bk = bank()
                    nc.scalar.activation(hid[:, kv, :], bk[:, 0:2 * NCMP], ACT.Silu).then_inc(hid_ready, 1)
                passing()
                bk = bank()
                nc.scalar.activation(kcz[0:64, 0, :], bk[0:64, 0:2 * NCMP], ACT.Copy)
                read(nc.scalar.activation(kcz[64:128, 1, :], bk[64:128, 0:2 * NCMP], ACT.Copy))
                passing()
                read(nc.scalar.activation(vcz[0:NCMP, :], bank()[0:NCMP, 0:128], ACT.Copy))
                for _ in range(3):
                    next_slab()
                attention(nsa_groups(), LEAD["nsa"])
                operand()
                turn(8)
                next_slab()
                ahead()

            def conformer():
                start_mixer()
                for _ in range(3):
                    next_slab()
                for j in range(8):
                    ready(j)
                    if j >= 2:
                        act.wait_ge(cu_done, 4 + j - 1)
                    nc.scalar.activation(silu[:, (j % 2) * T:(j % 2 + 1) * T], bank()[:, T:2 * T], ACT.Sigmoid,
                                         bias=v("b_pw1", 8 + j)).then_inc(u_copied, 1)
                    next_slab()
                for k in range(KD):
                    act.wait_ge(cen_ready, k + 1)
                    nc.scalar.activation(hf[:, k, :], qT[:, k, :], ACT.Square).then_inc(sq_ready, 1)
                operand()
                for k in range(KD + 1):
                    if k < KD:
                        act.wait_ge(ln_u, k + 1)
                        nc.scalar.activation(kT[:, k, :], hf[:, k, :], ACT.Silu, bias=v("ln_b", k)).then_inc(ln_silu, 1)
                    if k:
                        act.wait_ge(ln_silu, k)
                        nc.scalar.activation(h_hi[:, k - 1, :], kT[:, k - 1, :], ACT.Copy).then_inc(hh_ready, 1)
                next_slab()
                ahead()

            def diff():
                start_mixer()
                for _ in range(3):
                    next_slab()
                for j in range(4):
                    ready(j)
                    read(nc.scalar.activation(qT[:, 2 * j:2 * j + 2, :].rearrange("p k t -> p (k t)"), bank(), ACT.Copy,
                                         scale=0.125))
                    next_slab()
                act.wait_ge(kt_zeroed, 2)
                for j in range(4, 8):
                    ready(j)
                    b3 = bank().rearrange("p (h t) -> p h t", h=2)
                    h = 2 * (j - 4)
                    nc.scalar.activation(kz[0:64, h:h + 2, 0, :], b3[0:64, :, :], ACT.Copy)
                    read(nc.scalar.activation(kz[64:128, h:h + 2, 1, :], b3[64:128, :, :], ACT.Copy))
                    next_slab()
                for j in range(8, 12):
                    ready(j)
                    at = (j - 8) * 2 * P
                    read(nc.scalar.activation(vt[:, :, at:at + 2 * P], bank().rearrange("p (a b) -> p a b", a=TT), ACT.Copy))
                    next_slab()
                passing()
                nc.scalar.activation(small[:, 6:8], bank()[:, 0:2], ACT.Exp, scale=float(P)).then_inc(lam_exp, 1)
                attention(diff_groups(), LEAD["diff"])
                operand()
                turn(8, gain_=gain[:, 0:1])
                next_slab()
                ahead()

            steps = {"begin": begin, "norm": norm, "ffn": ffn, "add": add, "final": final, "hybrid": hybrid, "nsa": nsa,
                     "conformer": conformer, "diff": diff}
            for kind, *a in plan:
                if kind in steps:
                    steps[kind](*a)

        @block.vector
        def _(dve):
            c = Count()

            def link(ins):
                n = c.take("link") + 1
                ins.then_inc(dve_link, 1)
                dve.wait_ge(dve_link, n)

            def split(slot, n):
                dve.wait_ge(hi_done[slot], n + 1)
                nc.vector.tensor_tensor(lo[slot][:, :], raw[slot][:, :], hi[slot][:, :].bitcast(F32),
                                        ALU.subtract).then_inc(lo_done[slot], 1)

            def next_slab():
                if c.get("ahead", 0):
                    c["ahead"] -= 1
                else:
                    j = c.take("slab")
                    split(j % 3, j // 3)

            def ahead(n=2):
                n = min(n, NSLAB - c.get("slab", 0))
                for _ in range(n):
                    next_slab()
                c["ahead"] = n

            def mac(buf, q, n):
                dve.wait_ge(ada_in_[buf], n * 16 + 16)
                if buf < 2:
                    w = ada_raw[:, buf, :].rearrange("p (k n) -> p k n", k=KD)
                    w = [w[:, k, :] for k in range(KD)]
                else:
                    w = [t[:, 2 * k:2 * k + 2, :].rearrange("p a b -> p (a b)") for t in
                         (kT[:, :, :], vt[:, :, :].rearrange("p a (b t) -> p (a b) t", t=T)) for k in range(KD // 2)]
                nc.vector.tensor_scalar(ada_acc[:, :], w[0], cact[:, 0:1], None, ALU.mult).then_inc(ada_mac, 1)
                for k in range(1, KD):
                    dve.wait_ge(ada_mac, q * KD + k)
                    nc.vector.scalar_tensor_tensor(ada_acc[:, :], w[k], cact[:, k:k + 1], ada_acc[:, :],
                                                   ALU.mult, ALU.add).then_inc(ada_mac, 1)

            def mod_out(q):
                dve.wait_ge(ada_cols, q + 1)
                at = q * PAIR
                b = vec[:, bass.ds(at + VEC["ada_b"][0], PAIR)]
                nc.vector.tensor_tensor(mod[:, bass.ds(at, PAIR)], M[:, 0:PAIR], b, ALU.add).then_inc(ada_mod, 1)

            def begin():
                nc.vector.memset(one[:, :], 1.0)
                for n, t in ones.items():
                    nc.vector.memset(t[:, :], 1.0 / n)
                nc.vector.memset(pr[:, :, :], 0.0)
                nc.vector.memset(small[:, :], 0.0)
                nc.vector.memset(zero_b[:, :], 0.0).then_inc(const_ready, 1)
                dve.wait_ge(act_ready, 1)
                mac(0, 0, 0)
                mod_out(0)
                dve.wait_ge(con_loaded, 16)
                con = hf[:, :, :].rearrange("p k t -> p (k t)")
                nc.vector.tensor_copy(ident[:, :], con[:, 0:P])
                nc.vector.tensor_copy(ident_b[:, :], con[:, 0:P])
                nc.vector.tensor_copy(causal_b[:, :], con[:, CON["causal"]:CON["causal"] + P])
                nc.vector.tensor_copy(dist_b[:, :, :].rearrange("p a b -> p (a b)"),
                                      con[:, CON["dist"]:CON["dist"] + TT * T])
                nc.vector.tensor_copy(cmp_b[:, :, :].rearrange("p a b -> p (a b)"),
                                      con[:, CON["cmp"]:CON["cmp"] + TT * NCMP])
                for h in range(8):
                    nc.vector.tensor_scalar(slope_b[:, h, :], con[:, 0:P], -SLOPES[h], None, ALU.mult)
                nc.vector.tensor_copy(small[:, 0:4], con[:, CON["row_ok"]:CON["row_ok"] + 4]
                                      ).then_inc(const_ready, 1)
                mac(1, 1, 0)
                rstd_of(EPS, copy=False)
                mod_out(1)
                mac(2, 2, 1)
                mod_out(2)
                mac(0, 3, 1)
                ahead(1)
                mod_out(3)
                c["ada0"] = 2

            def rope_angles():
                pi = math.pi
                big = 1.5 * 2.0 ** 23
                c1 = 6.28125
                c2 = 2 * pi - c1
                ang, turns, cos_in = qT[:, 1, :], qT[:, 2, :], qT[:, 3, :]
                dve.wait_ge(pos_loaded, 16)
                dve.wait_ge(const_ready, 2)
                link(nc.vector.tensor_copy(ang, qT[:, 0, :].bitcast(I32)))
                link(nc.vector.tensor_scalar(ang, ang, small[:, 2:3], None, ALU.mult))
                link(nc.vector.tensor_scalar(turns, ang, 1 / (2 * pi), big, ALU.mult, ALU.add))
                link(nc.vector.tensor_scalar(turns, turns, -big, None, ALU.add))
                link(nc.vector.scalar_tensor_tensor(ang, turns, -c1, ang, ALU.mult, ALU.add))
                link(nc.vector.scalar_tensor_tensor(ang, turns, -c2, ang, ALU.mult, ALU.add))
                top = float(np.nextafter(np.float32(pi), np.float32(0)))
                link(nc.vector.tensor_scalar(ang, ang, top, -top, ALU.min, ALU.max))
                link(nc.vector.scalar_tensor_tensor(cos_in, ang, -1.0, ang, ALU.mult, ALU.max))
                nc.vector.tensor_scalar(cos_in, cos_in, -1.0, pi / 2, ALU.mult, ALU.add).then_inc(rope_in, 1)

            def rsqrt(y, value, t, done=None):
                link(nc.vector.tensor_scalar(y.bitcast(I32), value.bitcast(I32), -0.5, float(0x5f3759df),
                                             ALU.mult, ALU.add))
                for step in range(3):
                    link(nc.vector.tensor_tensor(t, value, y, ALU.mult))
                    link(nc.vector.scalar_tensor_tensor(t, t, -0.5, y, ALU.mult, ALU.mult))
                    last = nc.vector.scalar_tensor_tensor(y, t, 1.5, y, ALU.add, ALU.mult)
                    if step == 2 and done is not None:
                        last.then_inc(done, 1)
                    else:
                        link(last)

            def rstd_of(eps, scale=None, copy=True):
                dve.wait_ge(stat_ready, c.take("stat") + 1)
                for t, bank_ in enumerate((M, N)):
                    nc.vector.tensor_scalar(var[:, t:t + 1], bank_[:, 0:1], eps, None, ALU.add).then_inc(dve_link, 1)
                dve.wait_ge(dve_link, c.take("link", 2) + 2)
                rsqrt(root[:, :], var[:, 0:TT], var[:, TT:2 * TT], root_ready if scale is None else None)
                if scale is not None:
                    nc.vector.tensor_scalar(root[:, :], root[:, :], scale, None, ALU.mult).then_inc(root_ready, 1)
                dve.wait_ge(rstd_ready, c["stat"])
                if copy:
                    link(nc.vector.tensor_copy(rstd[:, :], N[:, 0:T]))

            def norm(n):
                if n < 6:
                    l, j = divmod(n, 3)
                    dve.wait_ge(ada_mod, c["mod"])
                    link(nc.vector.scalar_tensor_tensor(gain[:, :], modv(l, 3 * j + 1, 0, KD), 1.0,
                                                        v("norm_g", n * KD, KD), ALU.add, ALU.mult))
                    g = gain[:, :]
                else:
                    l, j = divmod(n - 6, 3)
                    g = v("mix_pre", l * KD, KD) if j == 1 else v("ffn_pre", (2 * l + j // 2) * KD, KD)
                if n:
                    rstd_of(EPS, copy=False)
                u0 = c.take("u", KD)
                hh0 = c.take("hh", KD)
                c.take("h", KD)
                for k in range(KD + 1):
                    if k < KD:
                        nc.vector.scalar_tensor_tensor(hf[:, k, :], x[:, k, :], g[:, k:k + 1], N[:, 0:T],
                                                       ALU.mult, ALU.mult).then_inc(u_ready, 1)
                    if k:
                        j = k - 1
                        dve.wait_ge(hh_ready, hh0 + k)
                        if n < 6:
                            ins = nc.vector.scalar_tensor_tensor(
                                h_lo[:, j, :], hf[:, j, :], modv(n // 3, 3 * (n % 3), j),
                                h_hi[:, j, :].bitcast(F32), ALU.add, ALU.subtract)
                        else:
                            ins = nc.vector.tensor_tensor(h_lo[:, j, :], hf[:, j, :], h_hi[:, j, :].bitcast(F32),
                                                          ALU.subtract)
                        ins.then_inc(h_ready, 1)

            def gate_mul(g, last_gf=True):
                dve.wait_ge(silu_done, g + 1)
                if last_gf:
                    dve.wait_ge(glo_done, g)
                nc.vector.tensor_tensor(gf[:, :], silu[:, :], AB[:, B, :], ALU.mult).then_inc(gf_done, 1)

            def gate_lo(g, to_hi=g_hi, to_lo=g_lo):
                dve.wait_ge(ghi_done, g + 1)
                nc.vector.tensor_tensor(to_lo[:, :], gf[:, :], to_hi[:, :].bitcast(F32), ALU.subtract
                                        ).then_inc(glo_done, 1)

            def ffn(f):
                q0, n_ada = ADA_FFN.get(f, (0, 0))
                a0 = c.take("ada0", n_ada)
                g0 = c.take("g", NSTEP)
                next_slab()
                next_slab()
                next_slab()
                (sa, na), (sb_, nb), (sw, nw) = step_slots(c.take("slab", 3 * NSTEP - 4) - 1)
                if f == 0:
                    rope_angles()
                if n_ada:
                    mac(0, q0, a0)

                def step(i, out_, mac_, a):
                    gate_mul(i + (g0 - 1), last_gf=not mac_)
                    split(sb_, i + nb)
                    split(sw, i + nw)
                    gate_lo(i + (g0 - 1))
                    if out_:
                        mod_out(i + (q0 - 1))
                    if a:
                        split(sa, i + (na + 1))
                    if mac_:
                        mac(0, i + q0, i + a0)

                for flags, run in groupby(range(1, NSTEP), lambda i: (i <= n_ada, i < n_ada, i < NSTEP - 1)):
                    run = list(run)
                    with dve.Fori(run[0], run[-1] + 1) as i:
                        step(i, *flags)
                gate_mul(g0 + NSTEP - 1)
                next_slab()
                gate_lo(g0 + NSTEP - 1, z_hi, z_lo)
                ahead()
                if n_ada == NSTEP:
                    mod_out(q0 + NSTEP - 1)
                if n_ada:
                    c["mod"] = q0 + n_ada

            def add(n):
                c.take("x_new", KD)
                half = 0.5 if n % 3 != 1 else 1.0
                if n < 6:
                    dve.wait_ge(ada_mod, c["mod"])
                    g_src = modv(n // 3, 3 * (n % 3) + 2, 0, KD)
                else:
                    l, j = divmod(n - 6, 3)
                    g_src = v("mix_post", l * KD, KD) if j == 1 else v("ffn_post", (2 * l + j // 2) * KD, KD)
                link(nc.vector.tensor_scalar(gate[:, :], g_src, half, None, ALU.mult))
                if n < 6:
                    for k in range(KD):
                        if k % 2 == 0:
                            result_bank(dve, c, n, k // 2)
                        nc.vector.scalar_tensor_tensor(x[:, k, :], Y[:, k, :], gate[:, k:k + 1], x[:, k, :],
                                                       ALU.mult, ALU.add).then_inc(x_new, 1)
                    return
                rstd_of(EPS)
                for k in range(KD + 1):
                    if k < KD:
                        bias = v("b_pw2", k) if n == 7 else 0.0
                        ins = nc.vector.scalar_tensor_tensor(hf[:, k, :], Y[:, k, :], bias, rstd[:, :],
                                                             ALU.add, ALU.mult)
                        ins.then_inc(dve_link, 1)
                        c.take("link")
                    if k:
                        dve.wait_ge(dve_link, c["link"] - (1 if k < KD else 0))
                        nc.vector.scalar_tensor_tensor(x[:, k - 1, :], hf[:, k - 1, :], gate[:, k - 1:k],
                                                       x[:, k - 1, :], ALU.mult, ALU.add).then_inc(x_new, 1)

            def final():
                c.take("x_new", KD)
                rstd_of(EPS)
                for k in range(KD):
                    nc.vector.scalar_tensor_tensor(x[:, k, :], x[:, k, :], v("final_g", k), rstd[:, :],
                                                   ALU.mult, ALU.mult).then_inc(x_new, 1)

            def start_mixer():
                c["base"] = c["slab"] - c["ahead"]

            def ready(j):
                j += c["base"]
                dve.wait_ge(used[j % 3], j // 3 + 1)

            def passing(n=1):
                dve.wait_ge(res_ready, c.take("passing", n) + n)

            def bank():
                return AB[:, c.take("res") % 2, :]

            def halves(bank_):
                return [bank_[:, 0:T], bank_[:, T:2 * T]]

            def reciprocals(bt, n):
                link(nc.vector.tensor_scalar(rec[:, 0:n], sums[:, bt % 3, 0:n], 1e-20, None, ALU.max))
                link(nc.vector.reciprocal(rec[:, 0:n], rec[:, 0:n]))

            def attention(groups, lead, batch, beside=None):
                n = len(groups)
                g0 = c.take("grp", n)
                b0 = c.take("batch", groups[-1]["batch"] + 1)
                for s_ in range(n + lead + 2):
                    if s_ < n:
                        G, gr = g0 + s_, groups[s_]
                        nu = len(gr["units"])
                        dve.wait_ge(s_ready, G + 1)
                        sc = score_bank(s_, lead).rearrange("p (u r) -> p u r", r=gr["room"])[:, 0:nu, 0:gr["nk"]]
                        nc.vector.tensor_reduce(nmax[:, G % 4, 0:nu], sc, AXX, ALU.max, negate=True
                                                ).then_inc(m_ready, 1)
                    if beside and s_ in beside:
                        beside[s_]()
                    if lead <= s_ < n + lead:
                        G, gr = g0 + s_ - lead, groups[s_ - lead]
                        dve.wait_ge(t_ready, G + 1)
                        if G >= 2:
                            dve.wait_ge(pv_done, G - 1)
                        w = len(gr["units"]) * gr["tiles"] * P
                        nc.vector.tensor_copy(pT[:, G % 2, 0:w], turn_bank(G)[:, 0:w]).then_inc(pt_ready, 1)
                    if s_ >= lead + 2:
                        g = s_ - lead - 2
                        if g == n - 1 or groups[g + 1]["batch"] != groups[g]["batch"]:
                            dve.wait_ge(pv_done, g0 + g + 1)
                            bt = groups[g]["batch"]
                            batch(bt, b0 + bt)

            def turn(n_chunks, gain_=None, first=0):
                for m in range(n_chunks // 2):
                    bk = bank()
                    dve.wait_ge(hh_ready, c["hh"] - KD + first + 2 * m + 2)
                    for cc in range(2):
                        k = first + 2 * m + cc
                        if gain_ is None:
                            ins = nc.vector.tensor_tensor(h_lo[:, k, :], halves(bk)[cc], h_hi[:, k, :].bitcast(F32),
                                                          ALU.subtract)
                        else:
                            ins = nc.vector.scalar_tensor_tensor(h_lo[:, k, :], halves(bk)[cc], gain_,
                                                                 h_hi[:, k, :].bitcast(F32), ALU.mult, ALU.subtract)
                        ins.then_inc(h_ready, 1)

            def hybrid():
                start_mixer()
                nc.vector.memset(cu[:, :, 0:2], 0.0)
                for _ in range(3):
                    next_slab()
                mac(0, ADA_MIX[0], c.take("ada0"))
                next_slab()
                mod_out(ADA_MIX[0])
                c.take("res", 2)
                rstd_of(EPS, scale=float(96 ** -0.5))
                for k in range(2):
                    nc.vector.scalar_tensor_tensor(gf[:, k * T:(k + 1) * T], vt[:, 0, k * T:(k + 1) * T],
                                                   v("q_norm", k), rstd[:, :], ALU.mult, ALU.mult).then_inc(lat_u, 1)
                dve.wait_ge(lat_hi, 2)
                nc.vector.tensor_tensor(g_lo[:, :], gf[:, :], g_hi[:, :].bitcast(F32), ALU.subtract
                                        ).then_inc(lat_ready, 1)
                rstd_of(EPS)
                nc.vector.scalar_tensor_tensor(hf[:, 3, :], vt[:, 1, 0:T], v("kv_norm"), rstd[:, :], ALU.mult,
                                               ALU.mult).then_inc(lat_u, 1)
                dve.wait_ge(rope_ready, 1)
                kr = vt[:, 1, T:2 * T]
                nc.vector.tensor_tensor(gf[64:96, 0:T], kr[96:128, :], sin_[96:128, :], ALU.mult)
                link(nc.vector.tensor_tensor(hf[64:96, 1, :], kr[64:96, :], cos_[64:96, :], ALU.mult))
                link(nc.vector.tensor_tensor(hf[64:96, 1, :], hf[64:96, 1, :], gf[64:96, 0:T], ALU.add))
                nc.vector.tensor_copy(kT[64:96, :, :], hf[64:96, 1, :].unsqueeze(1).to_broadcast([32, 8, T]))
                dve.wait_ge(lat_hi, 3)
                nc.vector.tensor_tensor(z_lo[:, 0:T], hf[:, 3, :], z_hi[:, 0:T].bitcast(F32), ALU.subtract
                                        ).then_inc(lat_ready, 1)
                next_slab()

                def conv(n):
                    dve.wait_ge(u_copied, c.take("cu") + 1)
                    nc.vector.tensor_tensor(cu[:, n, 2:T + 2], silu[:, (n % 2) * T:(n % 2 + 1) * T], bank()[:, T:2 * T],
                                            ALU.mult).then_inc(cu_done, 1)
                    dve.wait_ge(cu_done, c["cu"])
                    y = hf[:, 4 + n, :]
                    link(nc.vector.tensor_scalar(y, cu[:, n, 0:T], v("hy_conv", n), None, ALU.mult))
                    for tap in (1, 2):
                        link(nc.vector.scalar_tensor_tensor(y, cu[:, n, tap:tap + T], v("hy_conv", tap * 4 + n), y,
                                                            ALU.mult, ALU.add))

                for n in range(3):
                    conv(n)
                    next_slab()
                mac(0, ADA_MIX[1], c.take("ada0"))
                mod_out(ADA_MIX[1])
                c["mod"] = ADA_MIX[1] + 1
                dve.wait_ge(rope_ready, 1)
                s2, c2 = (a.unsqueeze(1).to_broadcast([32, 2, T]) for a in (sin_[96:128, :], cos_[64:96, :]))
                for h in range(0, 8, 2):
                    passing() if h < 6 else ready(5)
                    bk = bank().rearrange("p (h t) -> p h t", h=2)
                    g3 = gf[64:96, :].rearrange("p (h t) -> p h t", h=2)
                    nc.vector.tensor_tensor(g3, bk[96:128, :, :], s2, ALU.mult)
                    nc.vector.tensor_tensor(qT[64:96, h:h + 2, :], bk[64:96, :, :], c2, ALU.mult
                                            ).then_inc(read_dve, 1)
                    dve.wait_ge(read_dve, c.take("read_d") + 1)
                    link(nc.vector.tensor_tensor(qT[64:96, h:h + 2, :], qT[64:96, h:h + 2, :], g3, ALU.add))
                next_slab()
                c.take("passing", 4)
                c.take("res", 4)
                for t in range(TT):
                    passing() if t == 0 else ready(6)
                    nc.vector.tensor_copy(vt[:, t, 0:512], bank()).then_inc(read_dve, 1)
                    c.take("read_d")
                next_slab()

                def batch(t, bt):
                    reciprocals(bt, 8)
                    nc.vector.tensor_tensor(ot[:, t, 0:512].rearrange("p (h n) -> p h n", h=8),
                                            out_bank(bt)[:, :].rearrange("p (h n) -> p h n", h=8),
                                            rec[:, 0:8].unsqueeze(2).to_broadcast([P, 8, 64]), ALU.mult
                                            ).then_inc(o_read, 1)

                def gate_b(m, j):
                    def run():
                        ready(j)
                        y = hf[:, 4 + 2 * m:6 + 2 * m, :].rearrange("p k t -> p (k t)")
                        nc.vector.tensor_tensor(y, bank(), y, ALU.mult).then_inc(yc_done, 1)
                        next_slab()
                    return run

                def last():
                    next_slab()

                attention(mla_groups(), LEAD["mla"], batch, {0: lambda: conv(3), 1: gate_b(0, 8), 2: gate_b(1, 9), 3: last})
                hh0 = c.take("hh", KD)
                c.take("h", KD)
                for k in range(4):
                    dve.wait_ge(hh_ready, hh0 + k + 1)
                    nc.vector.tensor_tensor(h_lo[:, k, :], hf[:, 4 + k, :], h_hi[:, k, :].bitcast(F32), ALU.subtract
                                            ).then_inc(h_ready, 1)
                turn(4, first=4)
                next_slab()
                ahead()

            def nsa():
                start_mixer()
                kt3 = kT[:, :, :].rearrange("p (g m) t -> p g m t", m=2)
                nc.vector.memset(kt3[0:64, :, 1, :], 0.0)
                nc.vector.memset(kt3[64:128, :, 0, :], 0.0).then_inc(kt_zeroed, 1)
                for _ in range(7):
                    next_slab()
                c.take("res", 4)
                for kv in range(2):
                    c.take("res")
                    dve.wait_ge(cmp_copied, kv + 1)
                    src = (silu, gf)[kv][:, :].rearrange("p (g n j s) -> p g j n s", g=2, j=8, s=2)
                    to = blocks[kv].rearrange("p (j n g) -> p g j n", n=NCMP, g=2)
                    for half in range(2):
                        at = kv * 32 + half * 16
                        pe_ = vec[:, VEC["pe"][0] + at:VEC["pe"][0] + at + 16:2].unsqueeze(2).to_broadcast([P, 8, NCMP])
                        for g in range(2):
                            ins = nc.vector.tensor_tensor(to[:, g, 8 * half:8 * half + 8, :],
                                                          src[:, g, :, half:half + NCMP, 0], pe_, ALU.add)
                    ins.then_inc(blk_ready, 1)
                    next_slab()
                for _ in range(2):
                    next_slab()
                c.take("res", 2)
                ready(8)
                nc.vector.tensor_copy(vt[:, :, 0:2 * P], bank().rearrange("p (a b) -> p a b", a=TT)
                                      ).then_inc(read_dve, 1)
                c.take("read_d")
                ready(9)
                nc.vector.tensor_tensor(gates[:, :, :], bank()[:, 0:96].rearrange("p (a b) -> p a b", a=TT),
                                        v("gate_b", 0, 48).unsqueeze(1).to_broadcast([P, TT, 48]), ALU.add
                                        ).then_inc(gate_in, 1)
                for kv in range(2):
                    dve.wait_ge(cmp_hi, kv + 1)
                    th, tl = ((g_hi, g_lo), (z_hi, z_lo))[kv]
                    nc.vector.tensor_tensor(tl[:, 0:32 * NCMP], blocks[kv], th[:, 0:32 * NCMP].bitcast(F32),
                                            ALU.subtract).then_inc(cmp_in, 1)
                next_slab()
                c.take("res", 4)
                c.take("passing", 2)
                for _ in range(3):
                    next_slab()
                dve.wait_ge(gate_ready, 1)

                def batch(b_, bt):
                    t, rest = divmod(b_, 6)
                    g, branch = divmod(rest, 3)
                    reciprocals(bt, 8)
                    gs = gates[:, t, :].rearrange("p (h b) -> p h b", b=3)[:, 8 * g:8 * g + 8, branch]
                    if branch == 0:
                        link(nc.vector.scalar_tensor_tensor(rec[:, 0:8], rec[:, 0:8], small[:, t:t + 1], gs,
                                                            ALU.mult, ALU.mult))
                    else:
                        link(nc.vector.tensor_tensor(rec[:, 0:8], rec[:, 0:8], gs, ALU.mult))
                    o = ot[:, t, g * 512:(g + 1) * 512]
                    to = o if branch == 0 else gf[:, :]
                    ins = nc.vector.tensor_tensor(to.rearrange("p (h n) -> p h n", h=8),
                                                  out_bank(bt)[:, :].rearrange("p (h n) -> p h n", h=8),
                                                  rec[:, 0:8].unsqueeze(2).to_broadcast([P, 8, 64]), ALU.mult)
                    if branch:
                        link(ins)
                        ins = nc.vector.tensor_tensor(o, o, gf[:, :], ALU.add)
                    ins.then_inc(o_read, 1)
                    dve.wait_ge(o_read, bt + 1)

                attention(nsa_groups(), LEAD["nsa"], batch)
                c.take("hh", KD)
                c.take("h", KD)
                turn(8)
                next_slab()
                ahead()

            def conformer():
                start_mixer()
                nc.vector.memset(upad[:, :, 0:15], 0.0)
                nc.vector.memset(upad[:, :, 15 + T:30 + T], 0.0)
                for _ in range(3):
                    next_slab()

                def taps(j):
                    n = taps_dve[j]
                    for tap in range(n):
                        for k in (j, j + 1):
                            src = upad[:, k, tap:tap + T]
                            at = c.take("link")
                            if tap == 0:
                                ins = nc.vector.tensor_scalar(qT[:, k, :], src, v("w_dw", k), v("b_dw", k), ALU.mult,
                                                              ALU.add)
                            else:
                                dve.wait_ge(dve_link, at - 1)
                                ins = nc.vector.scalar_tensor_tensor(qT[:, k, :], src, v("w_dw", tap * KD + k),
                                                                     qT[:, k, :], ALU.mult, ALU.add)
                            ins.then_inc(dve_link, 1)
                    dve.wait_ge(dve_link, c["link"])
                    for k in (j, j + 1):
                        dve.wait_ge(dw_part, 2 * (k // 2) + 2)
                        nc.vector.tensor_tensor(qT[:, k, :], qT[:, k, :], Y[:, k, :], ALU.add).then_inc(dw_done, 1)

                for j in range(8):
                    dve.wait_ge(u_copied, c.take("cu") + 1)
                    nc.vector.scalar_tensor_tensor(upad[:, j, 15:15 + T], bank()[:, 0:T], v("b_pw1", j),
                                                   silu[:, (j % 2) * T:(j % 2 + 1) * T], ALU.add, ALU.mult
                                                   ).then_inc(cu_done, 1)
                    next_slab()
                    if j % 2:
                        dve.wait_ge(cu_done, c["cu"])
                        taps(j - 1)
                dve.wait_ge(mean_ready, 1)
                mu = gf[:, 0:T]
                link(nc.vector.tensor_copy(mu, N[:, 0:T]))
                for k in range(KD):
                    nc.vector.tensor_tensor(qT[:, k, :], qT[:, k, :], mu, ALU.subtract).then_inc(cen_ready, 1)
                rstd_of(1e-5)
                hh0 = c.take("hh", KD)
                c.take("h", KD)
                for k in range(KD):
                    nc.vector.scalar_tensor_tensor(hf[:, k, :], qT[:, k, :], v("ln_g", k), rstd[:, :], ALU.mult,
                                                   ALU.mult).then_inc(ln_u, 1)
                for k in range(KD):
                    dve.wait_ge(hh_ready, hh0 + k + 1)
                    nc.vector.tensor_tensor(h_lo[:, k, :], kT[:, k, :], h_hi[:, k, :].bitcast(F32), ALU.subtract
                                            ).then_inc(h_ready, 1)
                next_slab()
                ahead()

            def diff():
                start_mixer()
                nc.vector.memset(kz[0:64, :, 1, :], 0.0)
                nc.vector.memset(kz[64:128, :, 0, :], 0.0).then_inc(kt_zeroed, 1)
                nc.vector.tensor_tensor(small[:, 4:6], v("lam", 0, 2), v("lam", 2, 2), ALU.mult).then_inc(lam_in, 1)
                link(nc.vector.tensor_scalar(gain[:, 0:1], v("subln"), 1.0 - LAMBDA_INIT, None, ALU.mult))
                for _ in range(15):
                    next_slab()
                c.take("res", 13)
                dve.wait_ge(lam_exp, 1)
                c.take("passing")
                link(nc.vector.tensor_scalar(small[:, 204:205], small[:, 7:8], small[:, 6:7], -LAMBDA_INIT,
                                             ALU.subtract, ALU.add))

                def head_norms(t):
                    sq = hf[:, 4 * t:4 * t + 4, :].rearrange("p k t -> p (k t)")
                    o = ot[:, t, :]
                    link(nc.vector.tensor_tensor(sq, o, o, ALU.mult))
                    link(nc.vector.tensor_reduce(rec[:, 0:8], sq.rearrange("p (h n) -> p h n", h=8), AXX, ALU.add))
                    link(nc.vector.tensor_scalar(var[:, 0:8], rec[:, 0:8], 1.0 / P, 1e-5, ALU.mult, ALU.add))
                    rsqrt(rec[:, 0:8], var[:, :], gf[:, 0:8])
                    nc.vector.tensor_tensor(o.rearrange("p (h n) -> p h n", h=8), o.rearrange("p (h n) -> p h n", h=8),
                                            rec[:, 0:8].unsqueeze(2).to_broadcast([P, 8, P]), ALU.mult
                                            ).then_inc(ot_ready, 1)

                def batch(b_, bt):
                    t, hp = divmod(b_, 4)
                    reciprocals(bt, 4)
                    link(nc.vector.tensor_scalar(rec[:, 1:4:2], rec[:, 1:4:2], small[:, 204:205], None, ALU.mult))
                    g4 = gf[:, :].rearrange("p (h n) -> p h n", h=4)
                    link(nc.vector.tensor_tensor(g4, out_bank(bt)[:, :].rearrange("p (h n) -> p h n", h=4),
                                                 rec[:, 0:4].unsqueeze(2).to_broadcast([P, 4, P]), ALU.mult))
                    nc.vector.tensor_tensor(ot[:, t, hp * 2 * P:(hp + 1) * 2 * P].rearrange("p (h n) -> p h n", h=2),
                                            g4[:, 0:4:2, :], g4[:, 1:4:2, :], ALU.add).then_inc(o_read, 1)
                    dve.wait_ge(o_read, bt + 1)

                attention(diff_groups(), LEAD["diff"], batch)
                head_norms(0)
                dve.wait_ge(ot_ready, 1)
                head_norms(1)
                c.take("hh", KD)
                c.take("h", KD)
                turn(8, gain_=gain[:, 0:1])
                next_slab()
                ahead()

            c["mod"] = 4
            steps = {"begin": begin, "norm": norm, "ffn": ffn, "add": add, "final": final, "hybrid": hybrid, "nsa": nsa,
                     "conformer": conformer, "diff": diff}
            for kind, *a in plan:
                if kind in steps:
                    steps[kind](*a)


def chunks_(a):
    a = np.ascontiguousarray(a).reshape(-1, P)
    return a.T


def slab_of(*cols):
    a = np.concatenate(cols, axis=1)
    if a.shape[1] < 2 * P:
        a = np.concatenate([a, np.zeros((D, 2 * P - a.shape[1]), a.dtype)], axis=1)
    return a.reshape(KD, P, 2 * P).transpose(1, 0, 2).reshape(P, SLAB)


def rows_slab(a):
    return a.reshape(2, P, D).transpose(1, 0, 2).reshape(P, SLAB)


def ffn_slabs(a, b, w):
    for i in range(NSTEP + 1):
        if i < NSTEP:
            yield slab_of(a[:, i * STEP:(i + 1) * STEP])
            yield slab_of(b[:, i * STEP:(i + 1) * STEP])
        if i:
            yield rows_slab(w[(i - 1) * STEP:i * STEP])


def wide(w):
    for j in range(w.shape[1] // (2 * P)):
        yield slab_of(w[:, j * 2 * P:(j + 1) * 2 * P])


def twice(a):
    return np.concatenate([a, a], axis=1)


def all_slabs(i):
    for layer in range(2):
        for half in range(2):
            w13 = i["ff_w13"][layer, half]
            if half:
                if layer == 0:
                    w = i["hy_w_in"][0]
                    u, gc, gb = w[:, 0:512], w[:, 512:1024], w[:, 1024:1536]
                    cq, ckv, kr = w[:, 1536:1792], w[:, 1792:1920], w[:, 1920:1952]
                    yield slab_of(cq)
                    yield slab_of(ckv, np.zeros((D, 64), w.dtype), kr, kr[:, 16:32], kr[:, 0:16])
                    for j in range(3):
                        yield slab_of(u[:, j * P:(j + 1) * P], gc[:, j * P:(j + 1) * P])
                    uq = i["hy_w_uq"][0].reshape(2, P, 8, 96)
                    uq = np.concatenate([uq, uq[..., 80:96], uq[..., 64:80]], axis=3)
                    yield uq.transpose(1, 0, 2, 3).reshape(P, SLAB)
                    yield np.concatenate([i["hy_w_ukv"][0], np.zeros((P, D), w.dtype)], axis=1)
                    yield slab_of(u[:, 3 * P:4 * P], gc[:, 3 * P:4 * P])
                    yield slab_of(gb[:, 0:2 * P])
                    yield slab_of(gb[:, 2 * P:4 * P])
                    yield from wide(i["hy_w_out"][0])
                else:
                    w = i["nsa_w_in"][0]
                    yield from wide(w[:, 0:1024])
                    kc, vc, ks, vs, kw, vw = (w[:, 1024 + n * P:1024 + (n + 1) * P] for n in range(6))
                    for a in (kc, vc, ks, kw):
                        yield slab_of(twice(a[:, 0:64]), twice(a[:, 64:128]))
                    yield slab_of(vs, vw)
                    yield slab_of(w[:, 1792:1840])
                    for kv in range(2):
                        yield i["nsa_cmp_w1"][0, kv].reshape(16, P, P).transpose(1, 0, 2).reshape(P, SLAB)
                    yield from wide(i["nsa_w_out"][0])
            yield from ffn_slabs(w13[:, 0:FF], w13[:, FF:], i["ff_w2"][layer, half])
    for layer in range(2):
        for half in range(2):
            if half:
                if layer == 0:
                    w = i["conv_w_pw1_2"][0]
                    for j in range(KD):
                        yield slab_of(w[:, j * P:(j + 1) * P], w[:, D + j * P:D + (j + 1) * P])
                    yield from wide(i["conv_w_pw2_2"][0])
                else:
                    yield from wide(i["attn_w_qkv_2"][0])
                    yield from wide(i["attn_w_o_2"][0])
            yield from ffn_slabs(i["ffn_w_gate_2"][layer, half], i["ffn_w_up_2"][layer, half],
                                 i["ffn_w_down_2"][layer, half])


def vectors(i):
    def rows(a):
        return np.concatenate([a, np.zeros((P - a.shape[0], a.shape[1]), a.dtype)], axis=0)

    pe = np.repeat(i["nsa_cmp_pe"][0].reshape(2, 16, P).reshape(32, P), 2, axis=0).T
    lam = rows(np.stack([i[f"attn_lambda_{n}_2"][0] for n in ("q1", "q2", "k1", "k2")], axis=1))
    parts = {
        "c": chunks_(i["c"]), "ada_b": chunks_(i["ada_b"]), "norm_g": chunks_(i["norm_g"]),
        "final_g": chunks_(i["final_g"]), "hy_conv": chunks_(i["hy_conv_w"]), "q_norm": chunks_(i["hy_q_norm"]),
        "kv_norm": chunks_(i["hy_kv_norm"]), "pe": pe, "ffn_pre": chunks_(i["ffn_norm_pre_2"]),
        "ffn_post": chunks_(i["ffn_norm_post_2"]), "mix_pre": chunks_(i["mix_norm_pre_2"]),
        "mix_post": chunks_(i["mix_norm_post_2"]), "b_pw1": chunks_(i["conv_b_pw1_2"]),
        "w_dw": chunks_(i["conv_w_dw_2"]), "b_dw": chunks_(i["conv_b_dw_2"]), "ln_g": chunks_(i["conv_ln_g_2"]),
        "ln_b": chunks_(i["conv_ln_b_2"]), "b_pw2": chunks_(i["conv_b_pw2_2"]), "subln": chunks_(i["attn_subln_g_2"]),
        "lam": lam, "gate_b": np.broadcast_to(i["nsa_gate_b"], (P, 48)),
        "cmp_w2k": twice(i["nsa_cmp_w2"][0, 0]), "cmp_w2v": i["nsa_cmp_w2"][0, 1],
    }
    for name, (_, n) in VEC.items():
        assert parts[name].shape == (P, n), name
    return np.concatenate([parts[name] for name in VEC], axis=1)


def layout(inputs):
    i = {k: np.asarray(a) for k, a in inputs.items()}
    ada = i["ada_w"].reshape(2, KD, P, NPAIR // 2, PAIR * P).transpose(0, 3, 2, 1, 4).reshape(NPAIR, P, 2 * SLAB)
    return {
        "x_t": np.ascontiguousarray(i["x"][0].T.reshape(KD, P, T).transpose(1, 0, 2)),
        "positions": i["positions"],
        "vectors": np.ascontiguousarray(vectors(i)),
        "constants": constants(),
        "ada": np.ascontiguousarray(ada),
        "slabs": np.stack(list(all_slabs(i))),
    }


def kernel(**inputs):
    import concourse.bacc as _bacc
    from concourse.bass_utils import run_bass_kernel_spmd as _run

    nc = _bacc.Bacc("TRN2", target_bir_lowering=False, num_devices=1)
    arrays = layout(inputs)
    args = [nc.dram_tensor(name, a.shape, mybir.dt.from_np(a.dtype), kind="ExternalInput").ap()
            for name, a in arrays.items()]
    out = nc.dram_tensor("out_t", (P, KD, T), F32, kind="ExternalOutput").ap()
    program(nc, *args, out)
    r = _run(nc, [arrays], core_ids=[0])
    return r.results[0]["out_t"].transpose(2, 1, 0).reshape(1, T, D)
```
